# Optimizing a Trainium2 kernel written in Bass

```python
import math
import jax, jax.numpy as jnp
from jax import lax
import numpy as np

D_MODEL = 1024
BATCH = 1
SEQ = 256
DEPTH = 2

GRID_W = 64
N_BRANCH = 4
BRANCH_W = 256
HEAD_DIM = 64

ATT_HEADS = 4
ATT_KV_HEADS = 2
ATT_BLOCK = 128
ROPE_THETA = 10000.0
QK_EPS = 1e-6

RW_HEADS = 4
RW_DECAY_LORA = 64
RW_A_LORA = 64
RW_G_LORA = 128
RW_GN_EPS = 64e-5
RW_SIZES = (BRANCH_W, BRANCH_W, BRANCH_W, RW_DECAY_LORA, RW_DECAY_LORA, RW_A_LORA, RW_G_LORA)
RW_COLS = sum(RW_SIZES)

S5_GROUP = 16
S5_GROUPS = BRANCH_W // S5_GROUP
S5_STATE = 64

ML_HEADS = 4
ML_CHUNK = 64
ML_CONV_W = 5

IN_SIZES = (ATT_HEADS * HEAD_DIM, ATT_KV_HEADS * HEAD_DIM, ATT_KV_HEADS * HEAD_DIM, RW_COLS, BRANCH_W,
            2 * BRANCH_W, BRANCH_W, 2 * ML_HEADS, 2 * ML_HEADS, BRANCH_W)
IN_COLS = sum(IN_SIZES)

D_FF = 2816
N_EXPERTS = 8
TOP_K = 2
D_FF_EXPERT = 3584
N_DENSE = (DEPTH + 1) // 2
N_MOE = DEPTH // 2

ALPHA = (2 * DEPTH) ** 0.25
BETA = (8 * DEPTH) ** -0.25
LN_EPS = 1e-5

kernel_name = 'hybrid_gated_parallel_encoder'

def _split(t, sizes):
    return jnp.split(t, np.cumsum(sizes)[:-1].tolist(), axis=-1)

def layer_norm(x, g, b):
    xf = x.astype(jnp.float32)
    mu = jnp.mean(xf, -1, keepdims=True)
    var = jnp.mean(jnp.square(xf - mu), -1, keepdims=True)
    return ((xf - mu) * lax.rsqrt(var + LN_EPS) * g + b).astype(x.dtype)

def rms_norm_heads(x, g):
    xf = x.astype(jnp.float32)
    return xf * lax.rsqrt(jnp.mean(jnp.square(xf), -1, keepdims=True) + QK_EPS) * g

def _rotate(x, pos):
    n = x.shape[-1] // 2
    inv_freq = jnp.power(ROPE_THETA, -jnp.arange(n, dtype=jnp.float32) / n)
    ang = pos[:, None] * inv_freq
    cos = jnp.cos(ang)[None, :, None, :]
    sin = jnp.sin(ang)[None, :, None, :]
    x1, x2 = x[..., :n], x[..., n:]
    return jnp.concatenate([x1 * cos - x2 * sin, x1 * sin + x2 * cos], -1)

def rope_2d(x, row, col):
    half = x.shape[-1] // 2
    return jnp.concatenate([_rotate(x[..., :half], row), _rotate(x[..., half:], col)], -1)

def attention_mixer(q, k, v, gq, gk):
    bsz, seq, _ = q.shape
    rows = seq // GRID_W
    r_idx, c_idx = jnp.meshgrid(jnp.arange(rows), jnp.arange(GRID_W), indexing='ij')
    row = r_idx.reshape(-1).astype(jnp.float32)
    col = c_idx.reshape(-1).astype(jnp.float32)
    group = ATT_HEADS // ATT_KV_HEADS
    q = rope_2d(rms_norm_heads(q.reshape(bsz, seq, ATT_HEADS, HEAD_DIM), gq), row, col).astype(v.dtype)
    k = rope_2d(rms_norm_heads(k.reshape(bsz, seq, ATT_KV_HEADS, HEAD_DIM), gk), row, col).astype(v.dtype)
    v = v.reshape(bsz, seq, ATT_KV_HEADS, HEAD_DIM)
    n_blk = seq // ATT_BLOCK
    q_blocks = q.reshape(bsz, n_blk, ATT_BLOCK, ATT_KV_HEADS, group, HEAD_DIM).transpose(1, 0, 3, 4, 2, 5)
    k_t = k.transpose(0, 2, 1, 3)
    v_t = v.transpose(0, 2, 1, 3)
    scale = HEAD_DIM ** -0.5

    def one_block(q_blk):
        s = jnp.einsum('bkgqd,bksd->bkgqs', q_blk, k_t, preferred_element_type=jnp.float32) * scale
        p = jax.nn.softmax(s, axis=-1)
        return jnp.einsum('bkgqs,bksd->bkgqd', p.astype(v_t.dtype), v_t)

    o = lax.map(one_block, q_blocks)
    return o.transpose(1, 0, 4, 2, 3, 5).reshape(bsz, seq, ATT_HEADS * HEAD_DIM)

def centred_token_shift(p, mix):
    prev = jnp.pad(p[:, :-1], ((0, 0), (1, 0), (0, 0)))
    nxt = jnp.pad(p[:, 1:], ((0, 0), (0, 1), (0, 0)))
    return p + mix[0] * (prev - p) + mix[1] * (nxt - p)

def _rwkv7_step(state, inp):
    r_t, w_t, k_t, v_t, kk_t, kka_t = inp
    sa = jnp.einsum('bhvk,bhk->bhv', state, -kk_t)
    state = state * w_t[:, :, None, :] + sa[..., None] * kka_t[:, :, None, :] + v_t[..., None] * k_t[:, :, None, :]
    return state, jnp.einsum('bhvk,bhk->bhv', state, r_t)

def rwkv7_mixer(p, mix, w0, w2, a0, a2, g2, k_k, k_a, r_k, gn_g, gn_b):
    bsz, seq, _ = p.shape
    f32 = jnp.float32
    p = centred_token_shift(p, mix)
    r, k, v, wd_f, wd_b, a_lo, g_lo = _split(p, RW_SIZES)
    heads = lambda t: t.astype(f32).reshape(bsz, seq, RW_HEADS, HEAD_DIM)
    a = heads(jax.nn.sigmoid((a0 + a_lo @ a2).astype(f32)))
    gate = jax.nn.sigmoid(g_lo) @ g2
    r, k, v = heads(r), heads(k), heads(v)
    kk = k * k_k.astype(f32).reshape(RW_HEADS, HEAD_DIM)
    kk = kk / jnp.maximum(jnp.sqrt(jnp.sum(kk * kk, -1, keepdims=True)), 1e-12)
    k = k * (1.0 + (a - 1.0) * k_a.astype(f32).reshape(RW_HEADS, HEAD_DIM))

    def decay(w_lo, w0_d, w2_d):
        w = -jax.nn.softplus(-(w0_d + jnp.tanh(w_lo) @ w2_d).astype(f32)) - 0.5
        return heads(jnp.exp(-jnp.exp(w)))

    time_major = lambda t: jnp.moveaxis(t, 1, 0)
    r_s, k_s, v_s, kk_s, kka_s = (time_major(t) for t in (r, k, v, kk, kk * a))
    state0 = jnp.zeros((bsz, RW_HEADS, HEAD_DIM, HEAD_DIM), f32)
    _, y_f = lax.scan(_rwkv7_step, state0, (r_s, time_major(decay(wd_f, w0[0], w2[0])), k_s, v_s, kk_s, kka_s))
    _, y_b = lax.scan(_rwkv7_step, state0, (r_s, time_major(decay(wd_b, w0[1], w2[1])), k_s, v_s, kk_s, kka_s), reverse=True)
    y = jnp.moveaxis(y_f + y_b, 0, 1)
    mu = jnp.mean(y, -1, keepdims=True)
    var = jnp.mean(jnp.square(y - mu), -1, keepdims=True)
    y = ((y - mu) * lax.rsqrt(var + RW_GN_EPS)).reshape(bsz, seq, BRANCH_W) * gn_g + gn_b
    bonus = jnp.sum(r * k * r_k.astype(f32), -1, keepdims=True) * v
    y = y + bonus.reshape(bsz, seq, BRANCH_W)
    return (y * gate).astype(p.dtype)

def _ssm_combine(left, right):
    a_l, b_l = left
    a_r, b_r = right
    return a_r * a_l, a_r * b_l + b_r

def s5_mixer(u, lam_re, lam_im, log_dt, b_re, b_im, c_re, c_im, d_skip, glu_w, glu_b):
    bsz, seq, _ = u.shape
    f32 = jnp.float32
    uf = u.astype(f32)
    u_c = uf.reshape(bsz, seq, S5_GROUPS, S5_GROUP).astype(jnp.complex64)
    b_c = lax.complex(b_re.astype(f32), b_im.astype(f32))
    y = uf * d_skip.astype(f32)
    for direction in range(2):
        lam = lax.complex(jnp.minimum(lam_re[direction].astype(f32), -1e-4), lam_im[direction].astype(f32))
        dt = jnp.exp(log_dt[direction].astype(f32))[:, None]
        lam_bar = jnp.exp(lam * dt)
        b_bar = ((lam_bar - 1.0) / lam)[..., None] * b_c
        bu = jnp.einsum('bsgc,gpc->bsgp', u_c, b_bar)
        a_el = jnp.broadcast_to(lam_bar, (1, seq, S5_GROUPS, S5_STATE))
        _, states = lax.associative_scan(_ssm_combine, (a_el, bu), reverse=(direction == 1), axis=1)
        y_dir = (jnp.einsum('bsgp,gcp->bsgc', states.real, c_re[direction].astype(f32))
                 - jnp.einsum('bsgp,gcp->bsgc', states.imag, c_im[direction].astype(f32)))
        y = y + y_dir.reshape(bsz, seq, BRANCH_W)
    y = jax.nn.gelu(y)
    y = y * jax.nn.sigmoid(y @ glu_w.astype(f32) + glu_b.astype(f32))
    return y.astype(u.dtype)

def centred_depthwise_conv(x, w, b):
    width = w.shape[0]
    y = lax.conv_general_dilated(x, w.astype(x.dtype)[:, None, :], window_strides=(1,),
                                 padding=[(width // 2, width // 2)],
                                 dimension_numbers=('NWC', 'WIO', 'NWC'),
                                 feature_group_count=x.shape[-1])
    return y + b

def mlstm_chunkwise(q, k, v, log_i, log_f):
    bsz, nh, seq, d = q.shape
    nc, L = seq // ML_CHUNK, ML_CHUNK
    q, k, v = (t.reshape(bsz, nh, nc, L, d) for t in (q, k, v))
    log_i, log_f = log_i.reshape(bsz, nh, nc, L), log_f.reshape(bsz, nh, nc, L)
    b = jnp.cumsum(log_f, axis=-1)
    g = b[..., -1]
    w_end = g[..., None] - b + log_i
    m_loc = jnp.max(w_end, -1)
    e = jnp.exp(w_end - m_loc[..., None])
    u_c = jnp.einsum('bhcl,bhcld,bhcle->bhcde', e, k, v)
    u_n = jnp.einsum('bhcl,bhcld->bhcd', e, k)

    def step(carry, xs):
        c_st, n_st, m = carry
        g_c, ml_c, uc_c, un_c = xs
        m_new = jnp.maximum(g_c + m, ml_c)
        a = jnp.exp(g_c + m - m_new)
        bb = jnp.exp(ml_c - m_new)
        new = (a[..., None, None] * c_st + bb[..., None, None] * uc_c, a[..., None] * n_st + bb[..., None] * un_c, m_new)
        return new, (c_st, n_st, m)

    init = (jnp.zeros((bsz, nh, d, d), jnp.float32), jnp.zeros((bsz, nh, d), jnp.float32), jnp.zeros((bsz, nh), jnp.float32))
    chunk_major = lambda t: jnp.moveaxis(t, 2, 0)
    _, (c_prev, n_prev, m_prev) = lax.scan(step, init, (chunk_major(g), chunk_major(m_loc), chunk_major(u_c), chunk_major(u_n)))
    c_prev, n_prev, m_prev = jnp.moveaxis(c_prev, 0, 2), jnp.moveaxis(n_prev, 0, 2), jnp.moveaxis(m_prev, 0, 2)
    log_inter = b + m_prev[..., None]
    lower = jnp.tril(jnp.ones((L, L), dtype=bool))
    log_intra = jnp.where(lower, b[..., :, None] - b[..., None, :] + log_i[..., None, :], -jnp.inf)
    m_row = jnp.maximum(log_inter, jnp.max(log_intra, -1))
    s = jnp.einsum('bhcjd,bhcsd->bhcjs', q, k) * jnp.exp(log_intra - m_row[..., None])
    inter = jnp.exp(log_inter - m_row)
    num = jnp.einsum('bhcjs,bhcse->bhcje', s, v) + inter[..., None] * jnp.einsum('bhcjd,bhcde->bhcje', q, c_prev)
    den = jnp.sum(s, -1) + inter * jnp.einsum('bhcjd,bhcd->bhcj', q, n_prev)
    h = num / jnp.maximum(jnp.abs(den), jnp.exp(-m_row))[..., None]
    return h.reshape(bsz, nh, seq, d)

def mlstm_mixer(qk, v, i_pre, f_pre, o_pre, conv_w, conv_b, i_bias, f_bias):
    bsz, seq, _ = v.shape
    f32 = jnp.float32
    qk = jax.nn.silu(centred_depthwise_conv(qk, conv_w, conv_b))
    q, k = _split(qk, (BRANCH_W, BRANCH_W))
    heads = lambda t: t.astype(f32).reshape(bsz, seq, ML_HEADS, HEAD_DIM).transpose(0, 2, 1, 3)
    q, k, vh = heads(q), heads(k) * HEAD_DIM ** -0.5, heads(v)
    gate_shape = (bsz, seq, 2, ML_HEADS)
    log_i = (i_pre.astype(f32).reshape(gate_shape) + i_bias.astype(f32)).transpose(2, 0, 3, 1)
    log_f = jax.nn.log_sigmoid(f_pre.astype(f32).reshape(gate_shape) + f_bias.astype(f32)).transpose(2, 0, 3, 1)
    h_fwd = mlstm_chunkwise(q, k, vh, log_i[0], log_f[0])
    flip = lambda t: jnp.flip(t, axis=2)
    h_bwd = flip(mlstm_chunkwise(flip(q), flip(k), flip(vh), flip(log_i[1]), flip(log_f[1])))
    h = (h_fwd + h_bwd).transpose(0, 2, 1, 3).reshape(bsz, seq, BRANCH_W)
    return (jax.nn.sigmoid(o_pre.astype(f32)) * h).astype(v.dtype)

def swiglu(t, w1, w3, w2):
    return (jax.nn.silu(t @ w1) * (t @ w3)) @ w2

def moe_swiglu(x, router, w1, w3, w2):
    bsz, seq, d = x.shape
    t = x.reshape(bsz * seq, d)
    logits = (t @ router).astype(jnp.float32)
    top_val, top_idx = lax.top_k(logits, TOP_K)
    probs = jax.nn.softmax(top_val, axis=-1)
    combine = jnp.sum(jax.nn.one_hot(top_idx, N_EXPERTS, dtype=jnp.float32) * probs[..., None], axis=1)
    out = jnp.zeros((bsz * seq, d), jnp.float32)
    for e in range(N_EXPERTS):
        out = out + combine[:, e:e + 1] * swiglu(t, w1[e], w3[e], w2[e])
    return out.astype(x.dtype).reshape(bsz, seq, d)

def setup_inputs(seed: int = 0) -> dict:
    key = jax.random.key(seed)
    keys = iter(jax.random.split(key, 64))
    f32 = jnp.float32

    def nrm(shape, scale):
        return jax.random.normal(next(keys), shape, f32) * scale

    def unif(shape, lo, hi):
        return jax.random.uniform(next(keys), shape, f32, lo, hi)

    L, D, W, G, P = DEPTH, D_MODEL, BRANCH_W, S5_GROUPS, S5_STATE
    return {
        'x': nrm((BATCH, SEQ, D), 1.0),
        'w_in': nrm((L, D, IN_COLS), D ** -0.5),
        'b_in': nrm((L, IN_COLS), 0.02),
        'att_gq': 1.0 + nrm((L, HEAD_DIM), 0.02),
        'att_gk': 1.0 + nrm((L, HEAD_DIM), 0.02),
        'rw_mix': unif((L, 2, RW_COLS), 0.0, 0.5),
        'rw_w0': jnp.linspace(-6.5, -1.5, W, dtype=f32) + nrm((L, 2, W), 0.1),
        'rw_w2': nrm((L, 2, RW_DECAY_LORA, W), 0.1 * RW_DECAY_LORA ** -0.5),
        'rw_a0': nrm((L, W), 0.1),
        'rw_a2': nrm((L, RW_A_LORA, W), RW_A_LORA ** -0.5),
        'rw_g2': nrm((L, RW_G_LORA, W), RW_G_LORA ** -0.5),
        'rw_kk': 0.85 + nrm((L, W), 0.02),
        'rw_ka': 1.0 + nrm((L, W), 0.02),
        'rw_rk': nrm((L, RW_HEADS, HEAD_DIM), 0.1),
        'rw_ln_g': 1.0 + nrm((L, W), 0.02),
        'rw_ln_b': nrm((L, W), 0.02),
        's5_lam_re': -0.5 + nrm((L, 2, G, P), 0.01),
        's5_lam_im': math.pi * jnp.arange(P, dtype=f32) + nrm((L, 2, G, P), 0.01),
        's5_log_dt': unif((L, 2, G), math.log(1e-3), math.log(1e-1)),
        's5_b_re': nrm((L, G, P, S5_GROUP), (2 * S5_GROUP) ** -0.5),
        's5_b_im': nrm((L, G, P, S5_GROUP), (2 * S5_GROUP) ** -0.5),
        's5_c_re': nrm((L, 2, G, S5_GROUP, P), (2 * P) ** -0.5),
        's5_c_im': nrm((L, 2, G, S5_GROUP, P), (2 * P) ** -0.5),
        's5_d': nrm((L, W), 1.0),
        's5_glu_w': nrm((L, W, W), W ** -0.5),
        's5_glu_b': nrm((L, W), 0.02),
        'ml_conv_w': nrm((L, ML_CONV_W, 2 * W), ML_CONV_W ** -0.5),
        'ml_conv_b': nrm((L, 2 * W), 0.02),
        'ml_ib': nrm((L, 2, ML_HEADS), 0.1),
        'ml_fb': jnp.linspace(3.0, 6.0, ML_HEADS, dtype=f32) + nrm((L, 2, ML_HEADS), 0.1),
        'w_gate': nrm((L, N_BRANCH, D, D), D ** -0.5),
        'b_gate': nrm((L, N_BRANCH, D), 0.02),
        'w_branch': nrm((L, N_BRANCH, W, D), W ** -0.5),
        'w_out': nrm((L, D, D), BETA * D ** -0.5),
        'ln1_g': 1.0 + nrm((L, D), 0.02),
        'ln1_b': nrm((L, D), 0.02),
        'ffn_w1': nrm((N_DENSE, D, D_FF), D ** -0.5),
        'ffn_w3': nrm((N_DENSE, D, D_FF), D ** -0.5),
        'ffn_w2': nrm((N_DENSE, D_FF, D), BETA * D_FF ** -0.5),
        'moe_router': nrm((N_MOE, D, N_EXPERTS), D ** -0.5),
        'moe_w1': nrm((N_MOE, N_EXPERTS, D, D_FF_EXPERT), D ** -0.5),
        'moe_w3': nrm((N_MOE, N_EXPERTS, D, D_FF_EXPERT), D ** -0.5),
        'moe_w2': nrm((N_MOE, N_EXPERTS, D_FF_EXPERT, D), BETA * D_FF_EXPERT ** -0.5),
        'ln2_g': 1.0 + nrm((L, D), 0.02),
        'ln2_b': nrm((L, D), 0.02),
    }

def reference(x, w_in, b_in, att_gq, att_gk, rw_mix, rw_w0, rw_w2, rw_a0, rw_a2, rw_g2, rw_kk, rw_ka, rw_rk,
              rw_ln_g, rw_ln_b, s5_lam_re, s5_lam_im, s5_log_dt, s5_b_re, s5_b_im, s5_c_re, s5_c_im, s5_d,
              s5_glu_w, s5_glu_b, ml_conv_w, ml_conv_b, ml_ib, ml_fb, w_gate, b_gate, w_branch, w_out,
              ln1_g, ln1_b, ffn_w1, ffn_w3, ffn_w2, moe_router, moe_w1, moe_w3, moe_w2, ln2_g, ln2_b):
    for l in range(DEPTH):
        p = x @ w_in[l] + b_in[l]
        att_q, att_k, att_v, p_rw, p_s5, ml_qk, ml_v, ml_i, ml_f, ml_o = _split(p, IN_SIZES)
        branches = (
            attention_mixer(att_q, att_k, att_v, att_gq[l], att_gk[l]),
            rwkv7_mixer(p_rw, rw_mix[l], rw_w0[l], rw_w2[l], rw_a0[l], rw_a2[l], rw_g2[l], rw_kk[l], rw_ka[l],
                        rw_rk[l], rw_ln_g[l], rw_ln_b[l]),
            s5_mixer(p_s5, s5_lam_re[l], s5_lam_im[l], s5_log_dt[l], s5_b_re[l], s5_b_im[l], s5_c_re[l],
                     s5_c_im[l], s5_d[l], s5_glu_w[l], s5_glu_b[l]),
            mlstm_mixer(ml_qk, ml_v, ml_i, ml_f, ml_o, ml_conv_w[l], ml_conv_b[l], ml_ib[l], ml_fb[l]),
        )
        merged = jnp.zeros_like(x)
        for n in range(N_BRANCH):
            merged = merged + jax.nn.sigmoid(x @ w_gate[l, n] + b_gate[l, n]) * (branches[n] @ w_branch[l, n])
        x = layer_norm(ALPHA * x + merged @ w_out[l], ln1_g[l], ln1_b[l])
        if l % 2 == 0:
            ff = swiglu(x, ffn_w1[l // 2], ffn_w3[l // 2], ffn_w2[l // 2])
        else:
            ff = moe_swiglu(x, moe_router[l // 2], moe_w1[l // 2], moe_w3[l // 2], moe_w2[l // 2])
        x = layer_norm(ALPHA * x + ff, ln2_g[l], ln2_b[l])
    return x


_drawn_inputs = setup_inputs


def setup_inputs(seed=0):
    import zlib

    import numpy as np

    out = dict(_drawn_inputs(seed))
    spreads = {}
    factors = {'att_gq': 8.0,
     'att_gk': 8.0,
     'rw_w2': 8.0,
     'rw_a0': 5.373,
     'rw_kk': 8.0,
     'rw_ka': 8.0,
     'rw_ln_g': 8.0,
     'rw_ln_b': 8.0,
     's5_lam_re': 64.0,
     's5_lam_im': 34.232,
     's5_log_dt': 36.512,
     's5_b_re': 40.84,
     's5_b_im': 42.672,
     's5_c_re': 45.888,
     's5_c_im': 48.496,
     's5_glu_b': 45.475,
     'ml_conv_b': 4.64,
     'ml_ib': 8.0,
     'b_gate': 8.0}
    for name, (base, spread) in spreads.items():
        noise = np.random.default_rng([zlib.crc32(name.encode()), seed]).standard_normal(out[name].shape)
        drawn = base * np.exp(spread * noise) if base else spread * noise
        out[name] = __import__('jax').numpy.asarray(drawn.astype(out[name].dtype))
    for name, factor in factors.items():
        out[name] = (out[name] * factor).astype(out[name].dtype)
    return out
```

```python
from contextlib import ExitStack

import numpy as np

import concourse.bass as bass
from concourse import mybir
from concourse.alu_op_type import AluOpType as ALU

F32 = mybir.dt.float32
I32 = mybir.dt.int32
U32 = mybir.dt.uint32
ACT = mybir.ActivationFunctionType
AX = mybir.AxisListType.X

P = 128
T = 256
TT = T // P
D = 1024
KT = D // P
DEPTH = 2
W = 256
NBR = 4
HD = 64
CH = 64
NCH = T // CH
DFF = 2816
NE = 8
DFE = 3584
S5T = 8
ALPHA = (2 * DEPTH) ** 0.25
CAP = 96
RING = 4
UNIT = 3 * KT * P
PITCH = T + 4
NTILE = 23
(Q0, K0, V0, R0, RK0, RV0, WD, GL, AIF, U0, MQ0, MV0, MO0) = (0, 2, 3, 4, 6, 8, 10, 11, 12, 13, 15, 19, 21)
ROW_I, ROW_F = 64, 96
IN_UNITS = [(j, min(3, NTILE - j)) for j in range(0, NTILE, 3)]
FF_STEPS = DFF // P
EX_STEPS = DFE // P
BIG = 1.0e30
MAGIC = 1.5 * 2.0 ** 23
DECAY = float(np.exp(-0.5))

PV = {}
for _name, _n in [("b_in", NTILE), ("gqk", 3), ("mix", 18), ("w0", 4), ("a0", 2), ("kk", 2), ("ka", 2), ("rk", 2),
                  ("lng", 2), ("lnb", 2), ("lre", 16), ("lim", 16), ("ldt", 16), ("s5d", 2), ("glub", 2),
                  ("convw", 20), ("convb", 4), ("ifb", 1), ("bgate", 32)]:
    PV[_name] = (sum(n for _, n in PV.values()), _n)
NPV = sum(n for _, n in PV.values())
PM = {}
for _name, _n in [("a2", W), ("g2", W), ("w2", W), ("bre", 2 * P), ("bim", 2 * P), ("cre", 512), ("cim", 512),
                  ("glu", 2 * W), ("router", KT * NE)]:
    PM[_name] = (sum(n for _, n in PM.values()), _n)
NPM = sum(n for _, n in PM.values())
CO = {}
for _name, _n in [("ident", P), ("mean64", P), ("sum64", P), ("rot", P), ("cos", T), ("sin", T), ("cmask", 4 * CH),
                  ("lmask", 12 * CH), ("reset", T), ("trow", T), ("win", 2 * 3 * P), ("before", P), ("ones", P),
                  ("cap", CAP), ("eye64", CH), ("e8", NE), ("eps", 8), ("zero", P)]:
    CO[_name] = (sum(n for _, n in CO.values()), _n)
NCO = sum(n for _, n in CO.values())


def constants():
    c = np.zeros((P, NCO), np.float32)

    def put(name, a):
        at, n = CO[name]
        c[:, at:at + n] = np.asarray(a, np.float32).reshape(P, n)

    p = np.arange(P)
    put("ident", np.eye(P))
    same = (p[:, None] // HD == p[None, :] // HD)
    put("mean64", same / HD)
    put("sum64", same)
    n = 16
    rot = np.zeros((P, P))
    for m in range(P):
        if m % 32 < n:
            rot[m + n, m] = -1.0
        else:
            rot[m - n, m] = 1.0
    put("rot", rot)
    freq = np.power(np.float32(10000.0), -np.arange(n, dtype=np.float32) / n).astype(np.float32)
    t = np.arange(T)
    pos = np.where(((p % 64) < 32)[:, None], (t // 64)[None, :], (t % 64)[None, :]).astype(np.float32)
    ang = (pos * freq[p % 16][:, None]).astype(np.float32)
    put("cos", np.cos(ang.astype(np.float64)))
    put("sin", np.sin(ang.astype(np.float64)))
    j, i = (p % CH)[:, None], np.arange(CH)[None, :]
    put("cmask", np.concatenate([j < i, j <= i, j > i, j >= i], 1))
    lm = []
    for d in range(2):
        for lev in range(6):
            s = 1 << lev
            pair = j // (2 * s) == i // (2 * s)
            lo, hi = (j, i) if d == 0 else (i, j)
            lm.append(pair & (lo // s % 2 == 0) & (hi // s % 2 == 1))
    put("lmask", np.concatenate(lm, 1))
    put("reset", np.broadcast_to((t % CH != 0), (P, T)))
    put("trow", np.broadcast_to(t, (P, T)))
    s, q = p[:, None], p[None, :]
    neg, zero = np.full((P, P), -BIG), np.zeros((P, P))
    put("win", np.concatenate([neg, np.where(s <= q, 0, -BIG), zero, zero, np.where(s >= q, 0, -BIG), neg], 1))
    put("before", s < q)
    put("ones", np.ones((P, P)))
    put("cap", np.broadcast_to(np.arange(CAP), (P, CAP)))
    put("eye64", j == i)
    put("e8", np.broadcast_to(np.arange(NE), (P, NE)))
    put("eps", np.broadcast_to([1e-6, 64e-5, 1e-5, np.pi / 2, 1.0, 0.0, 0.0, 0.0], (P, 8)))
    return c


def bc(ap, axis, n):
    a = ap.unsqueeze(axis)
    shape = list(a.shape)
    shape[axis] = n
    return a.to_broadcast(shape)


def encoder(nc, A):
    with ExitStack() as ctx:
        def sb(name, shape, dt=F32):
            return ctx.enter_context(nc.sbuf_tensor(name, shape, dt))

        def sem(name):
            return ctx.enter_context(nc.semaphore(name))

        banks = [ctx.enter_context(nc.psum_tensor(f"bank{i}", [P, 512], F32)) for i in range(8)]
        RB = 6
        ring = sb("ring", [P, RING, UNIT])
        x_tok = sb("x_tok", [P, TT, D])
        xT = sb("xT", [P, KT, T])
        brT = sb("brT", [P, NBR, 2, T])
        cst = sb("cst", [P, NCO])
        pv = sb("pv", [P, NPV])
        pm = sb("pm", [P, NPM])
        proj = sb("proj", [P, NTILE, PITCH])
        small = sb("small", [P, 128])
        n_pass = sb("n_pass", [P, 1], I32)
        ro_idx = sb("ro_idx", [P, TT, 8], U32)
        ARENA = 19300
        arena = sb("arena", [P, ARENA])

        def area(at, *shape):
            n = int(np.prod(shape))
            assert at + n <= ARENA, (at, shape)
            v = arena[:, at:at + n]
            if len(shape) == 1:
                return v
            names = "abcde"[:len(shape)]
            return v.rearrange(f"p ({' '.join(names)}) -> p {' '.join(names)}", **dict(zip(names, shape)))

        def C(name, k=0, n=None):
            at, m = CO[name]
            return cst[:, at + k:at + (m if n is None else k + n)]

        def V(name, k=0, n=1):
            at, _ = PV[name]
            return pv[:, at + k:at + k + n]

        def M(name, k=0, n=None):
            at, m = PM[name]
            return pm[:, at + k:at + (m if n is None else k + n)]

        ident = C("ident")
        EPS6, EPSG, EPSL, HALFPI = (C("eps", k, 1) for k in range(4))

        S = {n: sem(n) for n in (
            "bank_filled", "act_freed", "dve_freed", "act_step", "dve_step", "x_loaded", "cst_loaded", "par_loaded",
            "lnp_loaded", "xT_ready", "p_ready", "pads_zeroed", "unit_used", "stored",
            "at_qg", "at_sq", "at_rs", "at_qr", "at_v", "at_max", "at_exp", "at_p", "at_pT", "at_done",
            "rw_params", "rw_scaled", "rw_shift", "rw_th", "rw_tg", "rw_sg", "rw_ta", "rw_tw", "rw_gate", "rw_kk",
            "rw_sq", "rw_ss", "rw_bonus", "rw_V", "rw_cum", "rw_exp", "rw_feat", "rw_tok", "rw_M", "rw_CT", "rw_P",
            "rw_X", "rw_XT", "rw_Z", "rw_U", "rw_Y", "rw_S", "rw_yc", "rw_ysq", "rw_rs", "rw_done",
            "s5_par", "s5_mag", "s5_c", "s5_bu", "s5_fr", "s5_cs", "s5_prod", "s5_read", "s5_poly", "s5_th", "s5_g",
            "s5_glu", "s5_done",
            "ml_conv", "ml_tanh", "ml_qk", "ml_f", "ml_ln", "ml_rows", "ml_col", "ml_v", "ml_S", "ml_D", "ml_E",
            "ml_W", "ml_em", "ml_h", "ml_done", "ml_o",
            "mg_gate", "mg_sum", "mg_done", "ln_sum", "ln_rs", "ln_done", "h_filled", "h_silu", "h_ready", "y_out",
            "ro_done", "ro_diff", "ro_exp", "sel_ready", "sel_T", "xg_filled", "xg_ready", "sc_filled", "sc_added",
            "wT_ready", "passes_ready", "rank_moved")}
        slot_loaded = [sem(f"slot{i}_loaded") for i in range(RING)]
        issued = {}

        def inc(ins, name):
            issued[name] = issued.get(name, 0) + 1
            return ins.then_inc(S[name], 1)

        def stepper(eng, own):
            def step(ins, name=None, hold=True):
                name = name or own
                inc(ins, name)
                if hold:
                    eng.wait_ge(S[name], issued[name])
            return step

        units = {}
        stream = []

        def slot(u):
            return ring[:, u % RING, :]

        def add_unit(key, src, shape):
            u = len(stream)
            n = int(np.prod(shape))
            names = "abc"[:len(shape)]
            dst = slot(u)[:, 0:n].rearrange(f"p ({' '.join(names)}) -> p {' '.join(names)}",
                                            **dict(zip(names, shape)))
            units[key] = u
            stream.append((key, src, dst))

        first_ff = {}
        for L in range(DEPTH):
            for k, (j, n) in enumerate(IN_UNITS):
                add_unit(("in", L, k), A["w_in"][L, j:j + n].rearrange("n p c -> p n c"), (n, D))
            for br in range(NBR):
                for k in range(4):
                    add_unit(("gate", L, br, k),
                             A["w_gate"][L, 8 * br + 2 * k:8 * br + 2 * k + 2].rearrange("n p c -> p n c"), (2, D))
                add_unit(("branch", L, br), A["w_branch"][L, br], (2, D))
            for k in range(4):
                add_unit(("out", L, k), A["w_out"][L, k], (2, D))
            first_ff[L] = len(stream)
            if L == 0:
                for s in range(FF_STEPS):
                    add_unit(("ff", s), A["ffn"][s].unsqueeze(1), (1, UNIT))

        def slot_uses(u):
            return u // RING + 1

        def unit_wait(pe, key):
            u = units[key]
            pe.wait_ge(slot_loaded[u % RING], 16 * slot_uses(u))
            return stream[u][2]

        jobs, job_at = [], {}
        unit_end = {}
        used_before = {}

        block = ctx.enter_context(nc.Block())
        at_qg, at_sq, at_rs = area(0, 3, T), area(768, 3, T), area(1536, 3, T)
        at_t, at_qr = area(2304, 3, T), area(3072, 3, T)
        at_v = area(3840, TT, P)
        at_p, at_pT = area(4096, 4, TT, T), area(6144, 4, TT, T)
        rw_sh = area(0, 9, T)
        rw_a, rw_gate, rw_kk, rw_kp = (area(2304 + 512 * k, 2, T) for k in range(4))
        rw_cin, rw_cex = area(4352, 4, T), area(5376, 4, T)
        rw_AR = area(6400, 4, NCH, 2, CH)
        rw_BT, rw_KT = area(8448, 4, T), area(9472, 4, T)
        rw_tot, rw_etot = area(10496, 4, NCH), area(10512, 4, NCH)
        rw_Bt, rw_Kt, rw_Vt = area(10528, 4, NCH, HD), area(11552, 4, NCH, HD), area(12576, 2, NCH, HD)
        rw_MM = area(13088, 4, NCH, 4, CH)
        rw_X, rw_XT = area(17184, 16, CH), area(18208, 16, CH)
        rw_P = rw_cin.rearrange("p a b -> p (a b)").rearrange("p (m c) -> p m c", m=16)
        rw_CT = rw_cex.rearrange("p a b -> p (a b)").rearrange("p (m c) -> p m c", m=16)
        rw_S = area(4352, 4, HD)
        rw_Z, rw_U, rw_T = area(4608, 4, HD), area(4864, 4, HD), area(5120, 4, HD)
        rw_Y = area(8448, 2, T)
        rw_yc, rw_q, rw_bon = area(8960, 2, T), area(9472, 2, T), area(9984, 2, T)
        s5_bu = area(0, S5T, 2, T)
        s5_fr, s5_rn = area(4096, 4, T), area(5120, 4, T)
        s5_cos, s5_sin = area(6144, 4, T), area(7168, 4, T)
        s5_zr, s5_zi = area(8192, 4, T), area(9216, 4, T)
        s5_t1, s5_t2 = area(10240, 4, T), area(11264, 4, T)
        s5_pr = [area(12288 + 1024 * k, 4, T) for k in range(4)]
        s5_cc = area(16384, 4, 512)
        s5_q = area(18432, 24, 16)
        s5_y, s5_g, s5_u = area(4096, 2, T), area(4608, 2, T), area(5120, 2, T)
        ml_y, ml_th, ml_qk = area(0, 4, T), area(1024, 4, T), area(2048, 4, T)
        ml_row = [area(3072 + T * k, T) for k in range(12)]
        ml_col, ml_em = area(6144, 4, 16), area(6208, 4, 4)
        ml_vt = area(6400, TT, 4, HD + 1)
        ml_S = area(7000, 2, 2, T)
        ml_E, ml_D, ml_W = area(8024, 2, 2, T), area(9048, 2, 2, T), area(10072, 2, 2, T)
        ml_h, ml_so, ml_dn = area(11096, TT, W), area(11608, 2, T), area(12120, 8)
        mg_gate = area(0, 4, 512)
        mg_t = area(2048, 512)
        merged = area(4096, KT, T)
        y_tok = area(6144, TT, D)
        ln_gb = area(8192, 2, D)
        ln_bs, ln_mv, ln_rstd = area(10240, TT, 2, 6), area(10264, TT, 2), area(10268, TT)
        ff_sl = area(10496, 2, T)
        ff_h = area(11008, 4, T)
        acc = area(0, TT, D)
        ys = area(2048, D)
        xg = area(3072, KT, CAP)
        sel, selw = area(3840, TT, CAP), area(4032, TT, CAP)
        selwT = area(4224, T)
        ro = area(4480, 40, 16)

        @block.tensor
        def _(pe):
            def open_bank(name, release):
                n = len(jobs)
                if n >= RB:
                    pe.wait_ge(S[jobs[n - RB][0]], jobs[n - RB][1])
                count = 1 + sum(r == release for r, _ in jobs)
                jobs.append((release, count))
                job_at[name] = n
                return banks[n % RB]

            def fill(ins):
                inc(ins, "bank_filled")

            mm = nc.tensor.matmul

            def unit_ends(key, name):
                unit_end[units[key]] = (name, issued[name])

            def transposed_x(call, ready):
                for g in range(4):
                    b = open_bank(("xT", call, g), "xT_ready")
                    if g == 0:
                        ready()
                    for k in range(2):
                        for tt in range(TT):
                            last = nc.tensor.transpose(b[:, k * T + tt * P:k * T + (tt + 1) * P],
                                                       x_tok[:, tt, (2 * g + k) * P:(2 * g + k + 1) * P], ident)
                    fill(last)

            def project(L):
                pe.wait_ge(S["xT_ready"], 4 * (2 * L + 1))
                j = 0
                for k, (j0, n) in enumerate(IN_UNITS):
                    w = unit_wait(pe, ("in", L, k))
                    for i in range(n):
                        if j % 2 == 0:
                            b = open_bank(("in", L, j // 2), "p_ready")
                        for kt in range(KT):
                            last = mm(b[:, (j % 2) * T:(j % 2 + 1) * T], w[:, i, kt * P:(kt + 1) * P], xT[:, kt, :],
                                      start=(kt == 0), stop=(kt == KT - 1))
                        bank_full = j % 2 == 1 or j == NTILE - 1
                        if bank_full:
                            fill(last)
                        if i == n - 1:
                            if not bank_full:
                                inc(last, "unit_used")
                            unit_ends(("in", L, k), "bank_filled" if bank_full else "unit_used")
                        j += 1

            def attention(L):
                pe.wait_ge(S["at_sq"], L + 1)
                b = open_bank(("ms", L, 0), "act_freed")
                fill(mm(b[:, :], C("mean64"), at_sq[:, 0:2, :].rearrange("p a b -> p (a b)"), start=True, stop=True))
                b = open_bank(("ms", L, 1), "act_freed")
                fill(mm(b[:, 0:T], C("mean64"), at_sq[:, 2, :], start=True, stop=True))
                pe.wait_ge(S["at_qg"], L + 1)
                b = open_bank(("rot", L, 0), "dve_freed")
                fill(mm(b[:, :], C("rot"), at_qg[:, 0:2, :].rearrange("p a b -> p (a b)"), start=True, stop=True))
                b = open_bank(("rot", L, 1), "dve_freed")
                fill(mm(b[:, 0:T], C("rot"), at_qg[:, 2, :], start=True, stop=True))
                b = open_bank(("v", L), "at_v")
                for tt in range(TT):
                    last = nc.tensor.transpose(b[:, tt * P:(tt + 1) * P], proj[:, V0, 2 + tt * P:2 + (tt + 1) * P],
                                               ident)
                fill(last)
                pe.wait_ge(S["at_qr"], L + 1)
                for n in range(4):
                    i, h = n // 2, 64 * (n % 2)
                    b = open_bank(("score", L, n), "at_exp")
                    for tt in range(TT):
                        last = mm(b[:, tt * T:(tt + 1) * T], at_qr[h:h + HD, i, tt * P:(tt + 1) * P],
                                  at_qr[h:h + HD, 2, :], start=True, stop=True)
                    fill(last)
                for n in range(4):
                    pe.wait_ge(S["at_p"], 4 * L + n + 1)
                    b = open_bank(("pT", L, n), "at_pT")
                    for st in range(2):
                        for tt in range(TT):
                            last = nc.tensor.transpose(b[:, st * T + tt * P:st * T + (tt + 1) * P],
                                                       at_p[:, n, tt, st * P:(st + 1) * P], ident)
                    fill(last)
                pe.wait_ge(S["at_v"], L + 1)
                for n in range(4):
                    h = 64 * (n % 2)
                    pe.wait_ge(S["at_pT"], 4 * L + n + 1)
                    b = open_bank(("att", L, n), "at_done")
                    for st in range(2):
                        last = mm(b[h:h + HD, 0:T], at_v[:, st, h:h + HD], at_pT[:, n, st, :],
                                  start=(st == 0), stop=(st == 1))
                    fill(last)

            def two(b):
                return b[:, :].rearrange("p (a b) -> p a b", a=2)

            def rwkv(L):
                pe.wait_ge(S["rw_shift"], L + 1)
                b = open_bank(("rwa", L), "rw_ta")
                for q in range(2):
                    last = mm(two(b)[:, q, :], M("a2", q * P, P)[0:64], rw_sh[0:64, 8, :], start=True, stop=True)
                fill(last)
                pe.wait_ge(S["rw_th"], L + 1)
                for d in range(2):
                    b = open_bank(("rww", L, d), "rw_tw")
                    for q in range(2):
                        last = mm(two(b)[:, q, :], M("w2", q * P, P)[64 * d:64 * d + 64],
                                  rw_sh[64 * d:64 * d + 64, 6, :], start=True, stop=True)
                    fill(last)
                pe.wait_ge(S["rw_sg"], L + 1)
                b = open_bank(("rwg", L), "rw_gate")
                for q in range(2):
                    last = mm(two(b)[:, q, :], M("g2", q * P, P), rw_sh[:, 7, :], start=True, stop=True)
                fill(last)
                pe.wait_ge(S["rw_sq"], L + 1)
                b = open_bank(("rwss", L), "rw_ss")
                fill(mm(b[:, :], C("sum64"), rw_gate2(), start=True, stop=True))
                pe.wait_ge(S["rw_bonus"], L + 1)
                b = open_bank(("rwb", L), "dve_freed")
                fill(mm(b[:, :], C("sum64"), rw_bonus_in(), start=True, stop=True))
                for q in range(2):
                    b = open_bank(("rwV", L, q), "rw_V")
                    for ch in range(NCH):
                        for h in (0, 64):
                            last = mm(b[h:h + 64, ch * 64:(ch + 1) * 64], rw_sh[h:h + 64, 4 + q, ch * CH:(ch + 1) * CH],
                                      ident[h:h + 64, h:h + 64], start=True, stop=True)
                    fill(last)
                pe.wait_ge(S["rw_feat"], L + 1)
                for k, src in enumerate((rw_BT, rw_KT)):
                    for dp in range(4):
                        b = open_bank(("rwt", L, k, dp), "rw_tok")
                        for ch in range(NCH):
                            for h in (0, 64):
                                last = mm(b[h:h + 64, ch * 64:(ch + 1) * 64], src[h:h + 64, dp, ch * CH:(ch + 1) * CH],
                                          ident[h:h + 64, h:h + 64], start=True, stop=True)
                        fill(last)
                for dp in range(4):
                    for cp in range(2):
                        b = open_bank(("rwM", L, dp, cp), "rw_M")
                        for c in range(2):
                            ch = 2 * cp + c
                            for k, src in enumerate((rw_BT, rw_KT)):
                                for h in (0, 64):
                                    last = mm(b[h:h + 64, (2 * c + k) * P:(2 * c + k + 1) * P],
                                              src[h:h + 64, dp, ch * CH:(ch + 1) * CH],
                                              rw_AR[h:h + 64, dp, ch, :, :].rearrange("p a b -> p (a b)"),
                                              start=True, stop=True)
                        fill(last)
                for lev in range(6):
                    for d in range(2):
                        n = 12 * L + 2 * lev + d
                        pe.wait_ge(S["rw_CT"], n + 1)
                        if lev:
                            pe.wait_ge(S["rw_X"], 10 * L + 2 * (lev - 1) + d + 1)
                        b = open_bank(("rwP", L, lev, d), "rw_P")
                        for m in range(8):
                            for h in (0, 64):
                                last = mm(b[h:h + 64, m * 64:(m + 1) * 64], rw_CT[h:h + 64, 8 * d + m, :],
                                          rw_X[h:h + 64, 8 * d + m, :], start=True, stop=True)
                        fill(last)
                    for d in range(2):
                        n = 12 * L + 2 * lev + d
                        pe.wait_ge(S["rw_P"], n + 1)
                        if lev:
                            pe.wait_ge(S["rw_XT"], n - 1)
                        if lev < 5:
                            b = open_bank(("rwQ", L, lev, d), "rw_X")
                            for m in range(8):
                                for h in (0, 64):
                                    last = mm(b[h:h + 64, m * 64:(m + 1) * 64], rw_XT[h:h + 64, 8 * d + m, :],
                                              rw_P[h:h + 64, 8 * d + m, :], start=True, stop=True)
                            fill(last)
                        b = open_bank(("rwQT", L, lev, d), "rw_XT")
                        for m in range(8):
                            for h in (0, 64):
                                last = mm(b[h:h + 64, m * 64:(m + 1) * 64], rw_P[h:h + 64, 8 * d + m, :],
                                          rw_XT[h:h + 64, 8 * d + m, :], start=True, stop=True)
                        fill(last)
                pe.wait_ge(S["rw_tok"], 8 * (L + 1))
                pe.wait_ge(S["rw_XT"], 12 * (L + 1))
                for s in range(NCH):
                    lanes = [(dp, (s if dp < 2 else NCH - 1 - s), h) for dp in range(4) for h in (0, 64)]
                    pe.wait_ge(S["rw_S"], NCH * L + s + 1)
                    b = open_bank(("rwZ", L, s), "rw_Z")
                    for dp, ch, h in lanes:
                        o = b[h:h + 64, dp * 64:(dp + 1) * 64]
                        mm(o, rw_AR[h:h + 64, dp, ch, 0, :], rw_S[h:h + 64, dp, :], start=True, stop=False)
                        last = mm(o, rw_MM[h:h + 64, dp, ch, 2, :], rw_Vt[h:h + 64, dp % 2, ch, :], start=False, stop=True)
                    fill(last)
                    pe.wait_ge(S["rw_Z"], NCH * L + s + 1)
                    b = open_bank(("rwU", L, s), "rw_U")
                    for dp, ch, h in lanes:
                        last = mm(b[h:h + 64, dp * 64:(dp + 1) * 64], rw_XT[h:h + 64, dp * 4 + ch, :],
                                  rw_Z[h:h + 64, dp, :], start=True, stop=True)
                    fill(last)
                    pe.wait_ge(S["rw_U"], NCH * L + s + 1)
                    if s < NCH - 1:
                        b = open_bank(("rwS", L, s), "dve_freed")
                        for dp, ch, h in lanes:
                            o = b[h:h + 64, dp * 64:(dp + 1) * 64]
                            mm(o, rw_Bt[h:h + 64, dp, ch, :], rw_U[h:h + 64, dp, :], start=True, stop=False)
                            last = mm(o, rw_Kt[h:h + 64, dp, ch, :], rw_Vt[h:h + 64, dp % 2, ch, :], start=False,
                                      stop=True)
                        fill(last)
                    b = open_bank(("rwY", L, s), "rw_Y")
                    for dp, ch, h in lanes:
                        o = b[h:h + 64, dp * 64:(dp + 1) * 64]
                        mm(o, rw_S[h:h + 64, dp, :], rw_AR[h:h + 64, dp, ch, 1, :], start=True, stop=False)
                        mm(o, rw_U[h:h + 64, dp, :], rw_MM[h:h + 64, dp, ch, 1, :], start=False, stop=False)
                        last = mm(o, rw_Vt[h:h + 64, dp % 2, ch, :], rw_MM[h:h + 64, dp, ch, 3, :], start=False,
                                  stop=True)
                    fill(last)
                pe.wait_ge(S["rw_Y"], NCH * (L + 1))
                b = open_bank(("rwmu", L), "dve_freed")
                fill(mm(b[:, :], C("mean64"), rw_Y.rearrange("p a b -> p (a b)"), start=True, stop=True))
                pe.wait_ge(S["rw_ysq"], L + 1)
                b = open_bank(("rwvar", L), "act_freed")
                fill(mm(b[:, :], C("mean64"), rw_q.rearrange("p a b -> p (a b)"), start=True, stop=True))

            def rw_gate2():
                return rw_cin.rearrange("p a b -> p (a b)")[:, 0:512]

            def rw_bonus_in():
                return rw_cin.rearrange("p a b -> p (a b)")[:, 512:1024]

            def s5(L):
                for i in range(S5T):
                    h = 32 * (i % 4)
                    b = open_bank(("bu", L, i), "s5_bu")
                    if i == 0:
                        pe.wait_ge(S["p_ready"], 12 * (L + 1))
                    for k, name in enumerate(("bre", "bim")):
                        last = mm(two(b)[:, k, :], M(name, (i // 4) * P, P)[h:h + 32],
                                  proj[h:h + 32, U0 + i // 4, 2:2 + T], start=True, stop=True)
                    fill(last)
                pe.wait_ge(S["s5_c"], L + 1)
                for d in range(2):
                    for half in range(2):
                        n = 4 * L + 2 * d + half
                        pe.wait_ge(S["s5_prod"], n + 1)
                        for k in range(4):
                            for i in range(4):
                                col = (0, 1, 2, 2)[k]
                                last = mm(banks[6 + half][32 * i:32 * i + 32, 0:T],
                                          s5_cc[:, col, (d * S5T + half * 4 + i) * 32:(d * S5T + half * 4 + i + 1) * 32],
                                          s5_pr[k][:, i, :], start=(d == 0 and k == 0), stop=(d == 1 and k == 3),
                                          skip_group_check=True)
                        inc(last, "s5_read")
                pe.wait_ge(S["s5_g"], L + 1)
                b = open_bank(("glu", L), "s5_glu")
                for q in range(2):
                    for ct in range(2):
                        last = mm(two(b)[:, q, :], M("glu", ct * W + q * P, P), s5_g[:, ct, :], start=(ct == 0),
                                  stop=(ct == 1))
                fill(last)

            def mlstm(L):
                pe.wait_ge(S["ml_rows"], L + 1)
                b = open_bank(("mlT", L), "ml_col")
                for k, row in enumerate((6, 7, 8, 9)):
                    for tt in range(TT):
                        last = nc.tensor.transpose(b[:, k * 16 + tt * 8:k * 16 + tt * 8 + 8],
                                                   ml_row[row][0:8, tt * P:(tt + 1) * P], ident[0:8, 0:8])
                fill(last)
                b = open_bank(("mlv", L), "ml_v")
                for tt in range(TT):
                    for ct in range(2):
                        last = nc.tensor.transpose(b[:, tt * W + ct * P:tt * W + (ct + 1) * P],
                                                   proj[:, MV0 + ct, 2 + tt * P:2 + (tt + 1) * P], ident)
                fill(last)
                pe.wait_ge(S["ml_qk"], L + 1)

                def scores(h):
                    o = 64 * (h % 2)
                    b = open_bank(("mlS", L, h), "ml_S")
                    for st in range(2):
                        last = mm(two(b)[:, st, :], ml_qk[o:o + 64, 2 + h // 2, st * P:(st + 1) * P],
                                  ml_qk[o:o + 64, h // 2, :], start=True, stop=True)
                    fill(last)
                    b = open_bank(("mlG", L, h), "ml_D")
                    for d in range(2):
                        r = 4 * d + h
                        last = mm(two(b)[:, d, :], ident[0:8, r:r + 1].to_broadcast([8, P]), ml_row[4 + d][0:8, :],
                                  start=True, stop=True)
                    fill(last)

                def reads(h):
                    b = open_bank(("mlh", L, h), "ml_h")
                    pe.wait_ge(S["ml_W"], 4 * L + h + 1)
                    for d in range(2):
                        for tt in range(TT):
                            for st in range(2):
                                last = mm(b[:, (2 * d + tt) * 65:(2 * d + tt + 1) * 65],
                                          ml_W[:, d, st, tt * P:(tt + 1) * P], ml_vt[:, st, h, :], start=(st == 0),
                                          stop=(st == 1))
                    fill(last)

                scores(0)
                pe.wait_ge(S["ml_v"], L + 1)
                for h in range(4):
                    if h < 3:
                        scores(h + 1)
                    reads(h)
                pe.wait_ge(S["ml_h"], 4 * (L + 1))
                b = open_bank(("mlo", L), "ml_done")
                for ct in range(2):
                    for tt in range(TT):
                        last = nc.tensor.transpose(b[:, ct * T + tt * P:ct * T + (tt + 1) * P],
                                                   ml_h[:, tt, ct * P:(ct + 1) * P], ident)
                fill(last)

            def merge(L):
                for br in range(NBR):
                    for k in range(4):
                        w = unit_wait(pe, ("gate", L, br, k))
                        b = open_bank(("gate", L, br, k), "mg_gate")
                        for q in range(2):
                            for kt in range(KT):
                                last = mm(two(b)[:, q, :], w[:, q, kt * P:(kt + 1) * P], xT[:, kt, :],
                                          start=(kt == 0), stop=(kt == KT - 1))
                        fill(last)
                        unit_ends(("gate", L, br, k), "bank_filled")
                    w = unit_wait(pe, ("branch", L, br))
                    if br == 0:
                        pe.wait_ge(S["ml_done"], L + 1)
                    for k in range(4):
                        b = open_bank(("br", L, br, k), "mg_sum")
                        for q in range(2):
                            for ct in range(2):
                                last = mm(two(b)[:, q, :], w[:, ct, (2 * k + q) * P:(2 * k + q + 1) * P],
                                          brT[:, br, ct, :], start=(ct == 0), stop=(ct == 1))
                        fill(last)
                    unit_ends(("branch", L, br), "bank_filled")

            def out_projection(L):
                b = [open_bank(("out", L, k), "dve_freed") for k in range(4)]
                pe.wait_ge(S["mg_done"], 4 * (L + 1))
                for u in range(4):
                    w = unit_wait(pe, ("out", L, u))
                    for c in range(2):
                        kt = 2 * u + c
                        for k in range(4):
                            last = mm(b[k][:, :], merged[:, kt, (k // 2) * P:(k // 2 + 1) * P],
                                      w[:, c, (k % 2) * 512:(k % 2 + 1) * 512], start=(kt == 0), stop=(kt == KT - 1),
                                      skip_group_check=True)
                            if kt == KT - 1:
                                fill(last)
                    if u < 3:
                        inc(last, "unit_used")
                    unit_ends(("out", L, u), "unit_used" if u < 3 else "bank_filled")

            def all_banks_free():
                for n in range(max(0, len(jobs) - RB), len(jobs)):
                    pe.wait_ge(S[jobs[n][0]], jobs[n][1])

            def h_products(w, rhs, n, bank):
                for g in range(2):
                    for kt in range(KT):
                        last = mm(bank[:, g * n:(g + 1) * n], w[:, (g * KT + kt) * P:(g * KT + kt + 1) * P],
                                  rhs[:, kt, :], start=(kt == 0), stop=(kt == KT - 1))
                last.then_inc(S["h_filled"], 1)

            def dense():
                all_banks_free()
                pe.wait_ge(S["xT_ready"], 8)
                assert (FF_STEPS - 2) % 4 == 0
                u0 = first_ff[0]
                assert u0 % RING == 0 and FF_STEPS % 4 == 2
                used_before["dense"] = issued["unit_used"]

                def hidden(s, i, first=True):
                    pe.wait_ge(slot_loaded[i], 16 * (u0 // RING + 1) + (s - i) * 4)
                    if not first:
                        pe.wait_ge(S["h_ready"], s - 1)
                    h_products(ring[:, i, :], xT, T, banks[i % 2])

                def down(s, i, last_step=False):
                    pe.wait_ge(S["h_ready"], s + 1)
                    for k in range(4):
                        last = mm(banks[2 + k][:, :], ff_h[:, i, (k // 2) * P:(k // 2 + 1) * P],
                                  ring[:, i, 2 * D + (k % 2) * 512:2 * D + (k % 2 + 1) * 512],
                                  start=False, stop=last_step, skip_group_check=True)
                    last.then_inc(S["unit_used"], 1)

                for k in range(4):
                    mm(banks[2 + k][:, :], C("zero"), cst[:, 0:512], start=True, stop=False, skip_group_check=True)
                hidden(0, 0)
                hidden(1, 1)
                down(0, 0)
                with pe.Fori(0, FF_STEPS - 2, 4) as s:
                    for i in range(4):
                        hidden(s + i + 2, (i + 2) % 4, first=False)
                        down(s + i + 1, (i + 1) % 4)
                down(FF_STEPS - 1, (FF_STEPS - 1) % 4, True)
                issued["unit_used"] += FF_STEPS

            def router():
                b = open_bank(("route",), "dve_freed")
                pe.wait_ge(S["xT_ready"], 16)
                for tt in range(TT):
                    for kt in range(KT):
                        last = mm(b[:, tt * NE:(tt + 1) * NE], xT[:, kt, tt * P:(tt + 1) * P],
                                  M("router", kt * NE, NE), start=(kt == 0), stop=(kt == KT - 1))
                fill(last)
                pe.wait_ge(S["ro_done"], 1)
                b = open_bank(("rank",), "dve_freed")
                mm(b[:, 0:NE], C("before"), ro[:, 0, 0:NE], start=True, stop=True)
                mm(b[:, NE:2 * NE], C("ones"), ro[:, 0, 0:NE], start=True, stop=False)
                mm(b[:, NE:2 * NE], C("before"), ro[:, 0, NE:2 * NE], start=False, stop=True)
                mm(b[:, 2 * NE:3 * NE], C("ones"), ro[:, 0, 0:NE], start=True, stop=False)
                fill(mm(b[:, 2 * NE:3 * NE], C("ones"), ro[:, 0, NE:2 * NE], start=False, stop=True))

            def experts():
                all_banks_free()
                pe.wait_ge(S["passes_ready"], 1)
                passes = pe.value_load(n_pass[0:1, 0:1], min_val=1, max_val=3)
                u0 = first_ff[1]
                h0 = FF_STEPS
                used_before["experts"] = issued["unit_used"]
                with pe.Fori(0, passes) as ps:
                    with pe.Fori(0, NE) as e:
                        it = pe.snap(ps * NE + e)
                        pe.wait_ge(S["sel_ready"], it + 1)
                        for tt in range(TT):
                            last = nc.tensor.transpose(banks[6][0:CAP, tt * P:(tt + 1) * P], selw[:, tt, :], ident)
                        last.then_inc(S["sel_T"], 1)
                        for g in range(2):
                            for k in range(4):
                                for tt in range(TT):
                                    last = mm(banks[g][:, k * CAP:(k + 1) * CAP],
                                              x_tok[:, tt, (4 * g + k) * P:(4 * g + k + 1) * P], sel[:, tt, :],
                                              start=(tt == 0), stop=(tt == 1))
                            last.then_inc(S["xg_filled"], 1)
                        pe.wait_ge(S["xg_ready"], 2 * it + 2)

                        def hidden(s):
                            i = (u0 + s) % RING
                            pe.wait_ge(slot_loaded[i], 16 * (EX_STEPS // RING) * it + 16 * slot_uses(u0 + s))
                            pe.wait_ge(S["h_ready"], h0 + EX_STEPS * it + s - 1) if s >= 2 else None
                            h_products(ring[:, i, :], xg, CAP, banks[s % 2])

                        def down(s):
                            i = (u0 + s) % RING
                            pe.wait_ge(S["h_ready"], h0 + EX_STEPS * it + s + 1)
                            for hf in range(2):
                                last = mm(banks[2 + hf][0:CAP, :], ff_h[:, s % 4, 0:CAP],
                                          ring[:, i, 2 * D + hf * 512:2 * D + (hf + 1) * 512],
                                          start=(s == 0), stop=(s == EX_STEPS - 1), skip_group_check=True)
                            last.then_inc(S["unit_used"], 1)

                        hidden(0)
                        for s in range(EX_STEPS):
                            if s + 1 < EX_STEPS:
                                hidden(s + 1)
                            down(s)
                        pe.wait_ge(S["y_out"], 2 * it + 2)
                        pe.wait_ge(S["wT_ready"], it + 1)
                        for k in range(4):
                            if k >= 2:
                                pe.wait_ge(S["sc_added"], 4 * it + k - 1)
                            mm(banks[4 + k % 2][:, :], selwT[0:CAP, (k // 2) * P:(k // 2 + 1) * P],
                               ys[0:CAP, (k % 2) * 512:(k % 2 + 1) * 512], start=True, stop=True)\
                                .then_inc(S["sc_filled"], 1)

            pe.wait_ge(S["cst_loaded"], 16)
            transposed_x(0, lambda: pe.wait_ge(S["x_loaded"], 16))
            for L in range(DEPTH):
                pe.wait_ge(S["par_loaded"], 32 * (L + 1))
                project(L)
                attention(L)
                rwkv(L)
                s5(L)
                mlstm(L)
                merge(L)
                out_projection(L)
                transposed_x(2 * L + 1, lambda: pe.wait_ge(S["ln_done"], 4 * L + 2))
                if L == 0:
                    dense()
                    transposed_x(2, lambda: pe.wait_ge(S["ln_done"], 4))
                else:
                    router()
                    experts()

        def bank_of(eng, key):
            n = job_at[key]
            eng.wait_ge(S["bank_filled"], n + 1)
            return banks[n % RB]

        def two(b):
            return b[:, :].rearrange("p (a b) -> p a b", a=2)

        def flat(a):
            return a.rearrange("p a b -> p (a b)")

        @block.scalar
        def _(act):
            step = stepper(act, "act_step")
            f = nc.scalar.activation

            def read_xT(call):
                for g in range(4):
                    b = bank_of(act, ("xT", call, g))
                    step(nc.scalar.copy(xT[:, 2 * g:2 * g + 2, :], two(b)), "xT_ready", hold=False)

            def project(L):
                if L == 0:
                    act.wait_ge(S["pads_zeroed"], 1)
                for k in range((NTILE + 1) // 2):
                    b = bank_of(act, ("in", L, k))
                    for q in range(2):
                        j = 2 * k + q
                        if j < NTILE:
                            ins = f(proj[:, j, 2:2 + T], two(b)[:, q, :], ACT.Identity, bias=V("b_in", j))
                    step(ins, "p_ready", hold=False)
                act.wait_ge(S["p_ready"], 12 * (L + 1))

            def attention(L):
                if L:
                    act.wait_ge(S["ln_done"], 4 * L)
                step(f(at_sq, proj[:, Q0:Q0 + 3, 2:2 + T], ACT.Square), "at_sq")
                b = bank_of(act, ("ms", L, 0))
                step(f(flat(at_rs[:, 0:2, :]), b[:, :], ACT.Ln, bias=EPS6), "act_freed")
                b = bank_of(act, ("ms", L, 1))
                step(f(at_rs[:, 2, :], b[:, 0:T], ACT.Ln, bias=EPS6), "act_freed")
                step(f(flat(at_rs), flat(at_rs), ACT.Exp, scale=-0.5), "at_rs")
                b = bank_of(act, ("v", L))
                step(nc.scalar.copy(flat(at_v), b[:, 0:T]), "at_v")
                for n in range(4):
                    b = bank_of(act, ("score", L, n))
                    act.wait_ge(S["at_max"], 4 * L + n + 1)
                    for tt in range(TT):
                        ins = f(at_p[:, n, tt, :], two(b)[:, tt, :], ACT.Exp, bias=small[:, 4 * n + tt:4 * n + tt + 1],
                                scale=HD ** -0.5, accum_out=small[:, 4 * n + 2 + tt:4 * n + 3 + tt])
                    step(ins, "at_exp", hold=False)
                for n in range(4):
                    b = bank_of(act, ("pT", L, n))
                    step(nc.scalar.copy(at_pT[:, n, :, :], two(b)), "at_pT", hold=False)

            def rwkv(L):
                act.wait_ge(S["at_done"], 4 * (L + 1))
                act.wait_ge(S["rw_params"], L + 1)
                for j in range(9):
                    ins = f(rw_sh[:, j, :], proj[:, R0 + j, 2:2 + T], ACT.Identity, scale=small[:, 32 + j:33 + j])
                step(ins, "rw_scaled")
                act.wait_ge(S["rw_shift"], L + 1)
                step(f(rw_sh[:, 6, :], rw_sh[:, 6, :], ACT.Tanh), "rw_th")
                step(f(rw_sh[:, 7, :], rw_sh[:, 7, :], ACT.Tanh, scale=0.5), "rw_tg")
                b = bank_of(act, ("rwa", L))
                for q in range(2):
                    ins = f(rw_a[:, q, :], two(b)[:, q, :], ACT.Tanh, scale=0.5, bias=small[:, 48 + q:49 + q])
                step(ins, "rw_ta")
                for d in range(2):
                    b = bank_of(act, ("rww", L, d))
                    for q in range(2):
                        ins = f(rw_cex[:, 2 * d + q, :], two(b)[:, q, :], ACT.Tanh, scale=0.5,
                                bias=small[:, 50 + 2 * d + q:51 + 2 * d + q])
                    step(ins, "rw_tw")
                b = bank_of(act, ("rwg", L))
                step(nc.scalar.copy(flat(rw_gate), b[:, :]), "rw_gate")
                act.wait_ge(S["rw_kk"], L + 1)
                step(f(flat(rw_cin)[:, 0:512], flat(rw_kk), ACT.Square), "rw_sq")
                b = bank_of(act, ("rwss", L))
                step(f(rw_AR.rearrange("p a b c d -> p (a b c d)")[:, 0:512], b[:, :], ACT.Sqrt), "rw_ss")
                for q in range(2):
                    b = bank_of(act, ("rwV", L, q))
                    step(nc.scalar.copy(rw_Vt[:, q, :, :].rearrange("p a b -> p (a b)"), b[:, 0:T]), "rw_V")
                act.wait_ge(S["rw_cum"], L + 1)
                for dp in range(4):
                    v = lambda a: a[:, dp, :].rearrange("p (c t) -> p c t", c=NCH)
                    f(rw_AR[:, dp, :, 0, :], v(rw_cex), ACT.Exp)
                    f(rw_AR[:, dp, :, 1, :], v(rw_cin), ACT.Exp)
                f(flat(rw_etot), flat(rw_tot), ACT.Exp)
                step(f(flat(rw_BT), flat(rw_cin), ACT.Exp, scale=-1.0), "rw_exp")
                for k, dst in enumerate((rw_Bt, rw_Kt)):
                    for dp in range(4):
                        b = bank_of(act, ("rwt", L, k, dp))
                        step(nc.scalar.copy(dst[:, dp, :, :].rearrange("p a b -> p (a b)"), b[:, 0:T]), "rw_tok")
                for lev in range(6):
                    for d in range(2):
                        b = bank_of(act, ("rwP", L, lev, d))
                        step(nc.scalar.copy(flat(rw_P[:, 8 * d:8 * d + 8, :]), b[:, :]), "rw_P")
                for s in range(NCH):
                    b = bank_of(act, ("rwZ", L, s))
                    step(nc.scalar.copy(flat(rw_Z), b[:, 0:T]), "rw_Z")
                    b = bank_of(act, ("rwU", L, s))
                    step(nc.scalar.copy(flat(rw_U), b[:, 0:T]), "rw_U")
                act.wait_ge(S["rw_yc"], L + 1)
                step(f(flat(rw_q), flat(rw_yc), ACT.Square), "rw_ysq")
                b = bank_of(act, ("rwvar", L))
                step(f(flat(rw_q), b[:, :], ACT.Ln, bias=EPSG), "act_freed")
                step(f(flat(rw_q), flat(rw_q), ACT.Exp, scale=-0.5), "rw_rs")

            def s5(L):
                act.wait_ge(S["rw_done"], L + 1)
                act.wait_ge(S["s5_par"], 3 * L + 1)
                q = lambda k: s5_q[:, k, :]
                step(f(q(1), V("ldt", 0, 16), ACT.Exp), "s5_mag")
                act.wait_ge(S["s5_par"], 3 * L + 2)
                step(f(q(5), q(2), ACT.Exp), "s5_mag")
                act.wait_ge(S["s5_par"], 3 * L + 3)
                step(f(q(9), q(8), ACT.Sin, scale=3.14159250), "s5_mag")
                step(f(q(11), q(8), ACT.Abs), None)
                step(f(q(10), q(11), ACT.Sin, scale=-3.14159250, bias=HALFPI), "s5_mag")
                for i in range(S5T):
                    b = bank_of(act, ("bu", L, i))
                    step(nc.scalar.copy(s5_bu[:, i, :, :], two(b)), "s5_bu", hold=False)
                for n in range(4):
                    act.wait_ge(S["s5_fr"], 4 * L + n + 1)
                    step(f(flat(s5_sin), flat(s5_fr), ACT.Sin, scale=6.2831850), None)
                    step(f(flat(s5_rn), flat(s5_fr), ACT.Abs), None)
                    step(f(flat(s5_cos), flat(s5_rn), ACT.Sin, scale=-6.2831850, bias=HALFPI), "s5_cs")
                act.wait_ge(S["s5_poly"], L + 1)
                step(f(flat(s5_g), flat(s5_g), ACT.Tanh, scale=0.7978845608028654), "s5_th")
                b = bank_of(act, ("glu", L))
                for k in range(2):
                    ins = f(s5_u[:, k, :], two(b)[:, k, :], ACT.Tanh, scale=0.25, bias=small[:, 56 + k:57 + k])
                step(ins, "s5_glu")

            def mlstm(L):
                act.wait_ge(S["ml_f"], L + 1)
                r = ml_row
                step(f(r[2][0:8, :], r[1][0:8, :], ACT.Abs))
                step(f(r[2][0:8, :], r[2][0:8, :], ACT.Exp, scale=-1.0))
                step(f(r[2][0:8, :], r[2][0:8, :], ACT.Ln, bias=C("eps", 4, 1)[0:8]), "ml_ln")
                act.wait_ge(S["ml_conv"], L + 1)
                step(f(flat(ml_th), flat(ml_y), ACT.Tanh, scale=0.5), "ml_tanh")
                step(f(ml_so, proj[:, MO0:MO0 + 2, 2:2 + T], ACT.Tanh, scale=0.5), "ml_o")
                act.wait_ge(S["ml_col"], L + 1)
                step(f(ml_em[:, :, :], ml_col[:, :, 8:12], ACT.Exp, scale=-1.0), "ml_em")
                b = bank_of(act, ("mlv", L))
                for tt in range(TT):
                    ins = nc.scalar.copy(ml_vt[:, tt, :, 0:HD],
                                         b[:, tt * W:(tt + 1) * W].rearrange("p (h c) -> p h c", h=4))
                step(ins, "ml_v", hold=False)
                for h in range(4):
                    b = bank_of(act, ("mlS", L, h))
                    if h >= 2:
                        act.wait_ge(S["ml_W"], 4 * L + h - 1)
                    step(f(ml_S[:, h % 2, :, :], two(b), ACT.Copy, scale=1.0 / 32), "ml_S", hold=False)
                    act.wait_ge(S["ml_D"], 4 * L + h + 1)
                    e = ml_E.rearrange("p a b c -> p (a b c)")
                    step(f(e, e, ACT.Exp), "ml_E", hold=False)

            def merge(L):
                for br in range(NBR):
                    for k in range(4):
                        b = bank_of(act, ("gate", L, br, k))
                        if br == 0 and k == 0:
                            act.wait_ge(S["ml_done"], L + 1)
                        if br:
                            act.wait_ge(S["mg_sum"], 16 * L + 4 * (br - 1) + k + 1)
                        for q in range(2):
                            ins = f(mg_gate[:, k, q * T:(q + 1) * T], two(b)[:, q, :], ACT.Tanh, scale=0.5,
                                    bias=small[:, 64 + 8 * br + 2 * k + q:65 + 8 * br + 2 * k + q])
                        step(ins, "mg_gate", hold=False)

            def norm(k):
                act.wait_ge(S["ln_sum"], k + 1)
                step(f(ln_rstd, ln_mv[:, :, 1], ACT.Ln, bias=EPSL))
                step(f(ln_rstd, ln_rstd, ACT.Exp, scale=-0.5), "ln_rs")

            def gate_hidden(s, i, n, bank, first=False):
                act.wait_ge(S["h_filled"], s + 1)
                if not first:
                    act.wait_ge(S["h_ready"], s - 1)
                f(ff_sl[:, i % 2, 0:n], bank[:, 0:n], ACT.Silu).then_inc(S["h_silu"], 1)

            def dense():
                for s in range(2):
                    gate_hidden(s, s, T, banks[s], first=True)
                with act.Fori(2, FF_STEPS, 2) as s:
                    for i in range(2):
                        gate_hidden(s + i, i, T, banks[i])

            def experts():
                act.wait_ge(S["passes_ready"], 1)
                passes = act.value_load(n_pass[0:1, 0:1], min_val=1, max_val=3)
                h0 = FF_STEPS
                with act.Fori(0, passes) as ps:
                    with act.Fori(0, NE) as e:
                        it = act.snap(ps * NE + e)
                        for g in range(2):
                            act.wait_ge(S["xg_filled"], 2 * it + g + 1)
                            nc.scalar.copy(flat(xg[:, 4 * g:4 * g + 4, :]), banks[g][:, 0:4 * CAP])\
                                .then_inc(S["xg_ready"], 1)
                        for s in range(EX_STEPS):
                            gate_hidden(h0 + EX_STEPS * it + s, s, CAP, banks[s % 2])
                        act.wait_ge(S["unit_used"], used_before["experts"] + EX_STEPS * it + EX_STEPS)
                        nc.scalar.copy(ys[0:CAP, 0:512], banks[2][0:CAP, :]).then_inc(S["y_out"], 1)
                        nc.scalar.copy(ys[0:CAP, 512:1024], banks[3][0:CAP, :]).then_inc(S["y_out"], 1)

            read_xT(0)
            for L in range(DEPTH):
                if L == 0:
                    act.wait_ge(S["cst_loaded"], 16)
                act.wait_ge(S["par_loaded"], 32 * (L + 1))
                project(L)
                attention(L)
                rwkv(L)
                s5(L)
                mlstm(L)
                merge(L)
                norm(2 * L)
                read_xT(2 * L + 1)
                if L == 0:
                    dense()
                    norm(1)
                    read_xT(2)
                else:
                    act.wait_ge(S["ro_diff"], 1)
                    step(f(ro[:, 4, 0:2], ro[:, 4, 0:2], ACT.Exp), "ro_exp")
                    experts()
                    norm(3)

        @block.vector
        def _(dve):
            step = stepper(dve, "dve_step")
            tt_, ts, stt, cp = (nc.vector.tensor_tensor, nc.vector.tensor_scalar, nc.vector.scalar_tensor_tensor,
                                nc.vector.tensor_copy)
            DIR2 = lambda a: a.rearrange("p (d q) t -> p d q t", d=2)

            def attention(L):
                dve.wait_ge(S["p_ready"], 12 * L + 2)
                for j in range(3):
                    ins = ts(at_qg[:, j, :], proj[:, Q0 + j, 2:2 + T], V("gqk", j), None, ALU.mult)
                step(ins, "at_qg")
                for n, (a, m) in enumerate(((0, 2), (2, 1))):
                    b = bank_of(dve, ("rot", L, n))
                    step(tt_(at_t[:, a:a + m, :], b[:, 0:m * T].rearrange("p (a b) -> p a b", a=m),
                             bc(C("sin"), 1, m), ALU.mult), "dve_freed")
                step(tt_(at_qr, at_qg, bc(C("cos"), 1, 3), ALU.mult))
                step(tt_(at_qr, at_qr, at_t, ALU.add))
                dve.wait_ge(S["at_rs"], L + 1)
                step(tt_(at_qr, at_qr, at_rs, ALU.mult), "at_qr")
                for n in range(4):
                    b = bank_of(dve, ("score", L, n))
                    mx = small[:, 4 * n:4 * n + 2]
                    step(nc.vector.tensor_reduce(mx, two(b), AX, ALU.max))
                    step(ts(mx, mx, -HD ** -0.5, None, ALU.mult), "at_max")
                for n in range(4):
                    dve.wait_ge(S["at_exp"], 4 * L + n + 1)
                    sm = small[:, 4 * n + 2:4 * n + 4]
                    step(nc.vector.reciprocal(sm, sm))
                    step(tt_(at_p[:, n, :, :], at_p[:, n, :, :], bc(sm, 2, T), ALU.mult), "at_p")
                for n in range(4):
                    h = 64 * (n % 2)
                    b = bank_of(dve, ("att", L, n))
                    step(cp(brT[h:h + 64, 0, n // 2, :], b[h:h + 64, 0:T]), "at_done")

            def params(L):
                mx = lambda k: V("mix", 9 * k, 9)
                s = small
                step(tt_(s[:, 32:41], mx(0), mx(1), ALU.add))
                step(ts(s[:, 32:41], s[:, 32:41], -1.0, 1.0, ALU.mult, ALU.add))
                step(ts(s[:, 48:50], V("a0", 0, 2), 0.5, None, ALU.mult))
                step(ts(s[:, 50:54], V("w0", 0, 4), 0.5, None, ALU.mult))
                step(ts(s[:, 56:58], V("glub", 0, 2), 0.5, None, ALU.mult))
                step(ts(s[:, 64:96], V("bgate", 0, 32), 0.5, None, ALU.mult), "rw_params")

            def rwkv(L):
                dve.wait_ge(S["p_ready"], 12 * (L + 1))
                dve.wait_ge(S["rw_scaled"], L + 1)
                for k, o in ((0, 1), (1, 3)):
                    for j in range(9):
                        ins = stt(rw_sh[:, j, :], proj[:, R0 + j, o:o + T], V("mix", 9 * k + j), rw_sh[:, j, :],
                                  ALU.mult, ALU.add)
                    step(ins, "rw_shift" if k else None)
                R_, K_, V_ = rw_sh[:, 0:2, :], rw_sh[:, 2:4, :], rw_sh[:, 4:6, :]
                dve.wait_ge(S["rw_tg"], L + 1)
                step(ts(rw_sh[:, 7, :], rw_sh[:, 7, :], 0.5, 0.5, ALU.mult, ALU.add), "rw_sg")
                for q in range(2):
                    ins = ts(rw_kk[:, q, :], K_[:, q, :], V("kk", q), None, ALU.mult)
                step(ins, "rw_kk")
                dve.wait_ge(S["rw_ta"], L + 1)
                step(ts(flat(rw_a), flat(rw_a), 0.5, 0.5, ALU.mult, ALU.add))
                for q in range(2):
                    ins = ts(rw_kp[:, q, :], rw_a[:, q, :], 1.0, V("ka", q), ALU.subtract, ALU.mult)
                step(ins)
                step(stt(flat(rw_kp), flat(rw_kp), 1.0, flat(K_), ALU.add, ALU.mult))
                bin_ = flat(rw_cin)[:, 512:1024].rearrange("p (q t) -> p q t", q=2)
                for q in range(2):
                    ins = stt(bin_[:, q, :], R_[:, q, :], V("rk", q), rw_kp[:, q, :], ALU.mult, ALU.mult)
                step(ins, "rw_bonus")
                dve.wait_ge(S["rw_ss"], L + 1)
                nrm = rw_AR.rearrange("p a b c d -> p (a b c d)")[:, 0:512]
                step(ts(nrm, nrm, 1e-12, None, ALU.max))
                step(nc.vector.reciprocal(nrm, nrm))
                step(stt(flat(rw_kk), flat(rw_kk), -1.0, nrm, ALU.mult, ALU.mult))
                step(stt(flat(rw_a), flat(rw_a), -1.0, flat(rw_kk), ALU.mult, ALU.mult))
                b = bank_of(dve, ("rwb", L))
                dve.wait_ge(S["rw_V"], 2 * (L + 1))
                step(tt_(flat(V_), b[:, :], flat(V_), ALU.mult), "dve_freed")
                dve.wait_ge(S["rw_tw"], 2 * (L + 1))
                step(ts(flat(rw_cex), flat(rw_cex), 1.0, -0.5 * DECAY, ALU.add, ALU.mult))
                for dp in range(4):
                    ins = nc.vector.tensor_tensor_scan(rw_cin[:, dp, :], C("reset"), rw_cex[:, dp, :], 0.0,
                                                       ALU.mult, ALU.add)
                step(ins)
                chunked = lambda a: a.rearrange("p q (c t) -> p q c t", c=NCH)
                step(cp(rw_tot, chunked(rw_cin)[:, :, :, CH - 1]))
                step(tt_(flat(rw_cex[:, 0:2, :]), flat(rw_cin[:, 0:2, :]), flat(rw_cex[:, 0:2, :]), ALU.subtract))
                for q in (2, 3):
                    ins = tt_(chunked(rw_cin)[:, q, :, :], bc(rw_tot[:, q, :], 2, CH), chunked(rw_cin)[:, q, :, :],
                              ALU.subtract)
                step(ins)
                step(tt_(flat(rw_kt_tmp()), flat(rw_cin[:, 2:4, :]), flat(rw_cex[:, 2:4, :]), ALU.add))
                step(cp(flat(rw_cex[:, 2:4, :]), flat(rw_cin[:, 2:4, :])))
                step(cp(flat(rw_cin[:, 2:4, :]), flat(rw_kt_tmp())), "rw_cum")
                dve.wait_ge(S["rw_exp"], L + 1)
                for d in range(2):
                    r = slice(2 * d, 2 * d + 2)
                    tt_(flat(rw_KT[:, r, :]), flat(rw_BT[:, r, :]), flat(rw_kp), ALU.mult)
                    for q in range(2):
                        v = lambda a: a[:, q, :].rearrange("p (c t) -> p c t", c=NCH)
                        tt_(rw_AR[:, 2 * d + q, :, 0, :], rw_AR[:, 2 * d + q, :, 0, :], v(rw_kk), ALU.mult)
                        tt_(rw_AR[:, 2 * d + q, :, 1, :], rw_AR[:, 2 * d + q, :, 1, :], v(R_), ALU.mult)
                step(cp(rw_X, bc(C("eye64"), 1, 16)))
                step(cp(rw_XT, bc(C("eye64"), 1, 16)))
                for d in range(2):
                    r = slice(2 * d, 2 * d + 2)
                    ins = tt_(flat(rw_BT[:, r, :]), flat(rw_BT[:, r, :]), flat(rw_a), ALU.mult)
                step(ins, "rw_feat")
                for dp in range(4):
                    for c2 in range(2):
                        b = bank_of(dve, ("rwM", L, dp, c2))
                        mask = C("cmask", 2 * CH * (dp // 2), 2 * CH)
                        step(tt_(rw_MM[:, dp, 2 * c2:2 * c2 + 2, :, :].rearrange("p c (k a) t -> p (c k) (a t)", k=2),
                                 b[:, :].rearrange("p (m c) -> p m c", m=4), bc(mask, 1, 4), ALU.mult), "rw_M",
                             hold=False)
                dve.wait_ge(S["rw_M"], issued["rw_M"])
                for lev in range(6):
                    for d in range(2):
                        dst = rw_CT[:, 8 * d:8 * d + 8, :]
                        src = rw_MM[:, 2 * d:2 * d + 2, :, 0, :].rearrange("p q c t -> p (q c) t")
                        step(tt_(dst, src, bc(C("lmask", (6 * d + lev) * CH, CH), 1, 8), ALU.mult), "rw_CT")
                    for d in range(2):
                        if lev < 5:
                            b = bank_of(dve, ("rwQ", L, lev, d))
                            x = flat(rw_X[:, 8 * d:8 * d + 8, :])
                            step(tt_(x, b[:, :], x, ALU.add), "rw_X")
                        b = bank_of(dve, ("rwQT", L, lev, d))
                        x = flat(rw_XT[:, 8 * d:8 * d + 8, :])
                        step(tt_(x, b[:, :], x, ALU.add), "rw_XT")
                step(nc.vector.memset(flat(rw_S), 0.0), "rw_S")
                for s in range(NCH):
                    ch = (s, NCH - 1 - s)
                    if s < NCH - 1:
                        b = bank_of(dve, ("rwS", L, s))
                        step(tt_(flat(rw_T), b[:, 0:T], flat(rw_S), ALU.add), "dve_freed")
                    b = bank_of(dve, ("rwY", L, s))
                    for d in range(2):
                        y = rw_Y[:, :, ch[d] * CH:(ch[d] + 1) * CH]
                        src = b[:, d * P:(d + 1) * P].rearrange("p (q t) -> p q t", q=2)
                        ins = cp(y, src) if s < 2 else tt_(y, src, y, ALU.add)
                        if d == 0:
                            step(ins)
                    step(ins, "rw_Y")
                    if s < NCH - 1:
                        for d in range(2):
                            ins = tt_(rw_S[:, 2 * d:2 * d + 2, :], rw_T[:, 2 * d:2 * d + 2, :],
                                      bc(rw_etot[:, 2 * d:2 * d + 2, ch[d]], 2, HD), ALU.mult)
                        step(ins, "rw_S")
                b = bank_of(dve, ("rwmu", L))
                step(tt_(flat(rw_yc), b[:, :], flat(rw_Y), ALU.subtract), "dve_freed")
                step(ts(flat(rw_yc), flat(rw_yc), -1.0, None, ALU.mult), "rw_yc")
                dve.wait_ge(S["rw_rs"], L + 1)
                step(tt_(flat(rw_yc), flat(rw_yc), flat(rw_q), ALU.mult))
                for q in range(2):
                    ins = ts(rw_yc[:, q, :], rw_yc[:, q, :], V("lng", q), V("lnb", q), ALU.mult, ALU.add)
                step(ins)
                step(tt_(flat(rw_yc), flat(rw_yc), flat(V_), ALU.add))
                step(tt_(flat(brT[:, 1, :, :]), flat(rw_yc), flat(rw_gate), ALU.mult), "rw_done")

            def rw_kt_tmp():
                return rw_KT[:, 0:2, :]

            def s5(L):
                q = lambda k: s5_q[:, k, :]
                step(ts(q(0), V("lre", 0, 16), -1e-4, None, ALU.min), "s5_par")
                dve.wait_ge(S["s5_mag"], 4 * L + 1)
                step(tt_(q(2), q(0), q(1), ALU.mult), "s5_par")
                step(tt_(q(3), V("lim", 0, 16), q(1), ALU.mult))
                step(ts(q(4), q(3), 0.15915494309189535 / 2, None, ALU.mult))
                step(ts(q(8), q(4), MAGIC, -MAGIC, ALU.add, ALU.add))
                step(tt_(q(8), q(4), q(8), ALU.subtract))
                step(ts(q(7), q(8), 2.0, None, ALU.mult))
                step(ts(q(6), q(7), MAGIC, -MAGIC, ALU.add, ALU.add))
                step(tt_(q(7), q(7), q(6), ALU.subtract))
                step(ts(q(7)[:, 8:16], q(7)[:, 8:16], -1.0, None, ALU.mult))
                step(ts(q(8), q(8), 2.0, None, ALU.mult), "s5_par")
                step(ts(q(12), q(2), -1.0, None, ALU.max))
                step(ts(q(13), q(12), 1.0 / 12, 1.0, ALU.mult, ALU.add))
                for n in range(11, 1, -1):
                    step(stt(q(13), q(13), 1.0 / n, q(12), ALU.mult, ALU.mult))
                    step(ts(q(13), q(13), 1.0, None, ALU.add))
                step(tt_(q(13), q(13), q(12), ALU.mult))
                dve.wait_ge(S["s5_mag"], 4 * L + 4)
                step(ts(q(14), q(2), -1.0, None, ALU.is_ge))
                step(ts(q(15), q(5), 1.0, None, ALU.subtract))
                step(tt_(q(13), q(13), q(15), ALU.subtract))
                step(tt_(q(13), q(13), q(14), ALU.mult))
                step(tt_(q(13), q(13), q(15), ALU.add))
                step(ts(q(5), q(13), 1.0, None, ALU.add))
                step(tt_(q(15), q(9), q(9), ALU.mult))
                step(ts(q(15), q(15), -2.0, None, ALU.mult))
                step(tt_(q(16), q(9), q(10), ALU.mult))
                step(stt(q(16), q(16), 2.0, q(5), ALU.mult, ALU.mult))
                step(stt(q(17), q(15), 1.0, q(13), ALU.add, ALU.mult))
                step(tt_(q(17), q(17), q(15), ALU.add))
                step(tt_(q(18), q(0), q(0), ALU.mult))
                step(tt_(q(19), V("lim", 0, 16), V("lim", 0, 16), ALU.mult))
                step(tt_(q(18), q(18), q(19), ALU.add))
                step(nc.vector.reciprocal(q(18), q(18)))
                step(tt_(q(20), q(17), q(0), ALU.mult))
                step(tt_(q(21), q(16), V("lim", 0, 16), ALU.mult))
                step(tt_(q(20), q(20), q(21), ALU.add))
                step(tt_(q(20), q(20), q(18), ALU.mult))
                step(tt_(q(21), q(16), q(0), ALU.mult))
                step(tt_(q(22), q(17), V("lim", 0, 16), ALU.mult))
                step(tt_(q(21), q(21), q(22), ALU.subtract))
                step(tt_(q(21), q(21), q(18), ALU.mult))
                c = lambda a: a.rearrange("p (n c) -> p n c", n=16)
                cc = lambda k: c(s5_cc[:, k, :])
                cre, cim = c(M("cre")), c(M("cim"))
                kr, ki = bc(q(20), 2, 32), bc(q(21), 2, 32)
                step(tt_(cc(0), cre, kr, ALU.mult))
                step(tt_(cc(3), cim, ki, ALU.mult))
                step(tt_(cc(0), cc(0), cc(3), ALU.subtract))
                step(ts(cc(1), cc(0), -1.0, None, ALU.mult))
                step(tt_(cc(2), cre, ki, ALU.mult))
                step(tt_(cc(3), cim, kr, ALU.mult))
                step(tt_(cc(2), cc(2), cc(3), ALU.add))
                step(ts(cc(2), cc(2), -1.0, None, ALU.mult), "s5_c")
                for n in range(4):
                    d, half = n // 2, n % 2
                    lane = d * S5T + half * 4
                    step(tt_(s5_rn, bc(C("trow"), 1, 4), bc(q(7)[:, lane:lane + 4], 2, T), ALU.mult))
                    step(ts(flat(s5_fr), flat(s5_rn), MAGIC, -MAGIC, ALU.add, ALU.add))
                    step(tt_(flat(s5_fr), flat(s5_rn), flat(s5_fr), ALU.subtract), "s5_fr")
                    if n == 0:
                        dve.wait_ge(S["s5_bu"], 8 * (L + 1))
                    dve.wait_ge(S["s5_cs"], 4 * L + n + 1)
                    br, bi = (s5_bu[:, 4 * half:4 * half + 4, k, :] for k in range(2))
                    step(tt_(s5_t1, br, s5_cos, ALU.mult), hold=False)
                    step(tt_(s5_t2, bi, s5_sin, ALU.mult))
                    step(tt_(s5_t1, s5_t1, s5_t2, ALU.add))
                    back = slice(None, None, -1) if d else slice(None)
                    for i in range(4):
                        nc.vector.tensor_tensor_scan(s5_zr[:, i, back], q(5)[:, lane + i:lane + i + 1].to_broadcast([P, T]),
                                                     s5_t1[:, i, back], 0.0, ALU.mult, ALU.add)
                    step(tt_(s5_t2, bi, s5_cos, ALU.mult))
                    step(tt_(s5_t1, br, s5_sin, ALU.mult))
                    step(tt_(s5_t2, s5_t2, s5_t1, ALU.subtract))
                    for i in range(4):
                        ins = nc.vector.tensor_tensor_scan(s5_zi[:, i, back],
                                                           q(5)[:, lane + i:lane + i + 1].to_broadcast([P, T]),
                                                           s5_t2[:, i, back], 0.0, ALU.mult, ALU.add)
                    step(ins)
                    if n:
                        dve.wait_ge(S["s5_read"], 4 * L + n)
                    tt_(s5_pr[0], s5_cos, s5_zr, ALU.mult)
                    tt_(s5_pr[1], s5_sin, s5_zi, ALU.mult)
                    tt_(s5_pr[2], s5_sin, s5_zr, ALU.mult)
                    step(tt_(s5_pr[3], s5_cos, s5_zi, ALU.mult), "s5_prod")
                dve.wait_ge(S["s5_read"], 4 * (L + 1))
                for k in range(2):
                    ins = stt(s5_y[:, k, :], proj[:, U0 + k, 2:2 + T], V("s5d", k), banks[6 + k][:, 0:T], ALU.mult,
                              ALU.add)
                step(ins)
                step(tt_(flat(s5_g), flat(s5_y), flat(s5_y), ALU.mult))
                step(ts(flat(s5_g), flat(s5_g), 0.044715, 1.0, ALU.mult, ALU.add))
                step(tt_(flat(s5_g), flat(s5_g), flat(s5_y), ALU.mult), "s5_poly")
                dve.wait_ge(S["s5_th"], L + 1)
                step(stt(flat(s5_g), flat(s5_g), 1.0, flat(s5_y), ALU.add, ALU.mult), "s5_g")
                dve.wait_ge(S["s5_glu"], L + 1)
                step(stt(flat(s5_u), flat(s5_u), 1.0, flat(s5_g), ALU.add, ALU.mult))
                step(ts(flat(brT[:, 2, :, :]), flat(s5_u), 0.25, None, ALU.mult), "s5_done")

            def mlstm(L):
                r = [x[0:8, :] for x in ml_row]
                step(ts(r[0], proj[ROW_I:ROW_I + 8, AIF, 2:2 + T], V("ifb")[ROW_I:ROW_I + 8], None, ALU.add))
                step(ts(r[1], proj[ROW_F:ROW_F + 8, AIF, 2:2 + T], V("ifb")[ROW_F:ROW_F + 8], None, ALU.add), "ml_f")
                for k in range(5):
                    for j in range(4):
                        src = proj[:, MQ0 + j, k:k + T]
                        w = V("convw", 5 * j + k)
                        if k == 0:
                            ins = ts(ml_y[:, j, :], src, w, V("convb", j), ALU.mult, ALU.add)
                        else:
                            ins = stt(ml_y[:, j, :], src, w, ml_y[:, j, :], ALU.mult, ALU.add)
                    step(ins, "ml_conv" if k == 4 else None)
                dve.wait_ge(S["ml_ln"], L + 1)
                step(stt(r[2], r[1], 0.0, r[2], ALU.min, ALU.subtract))
                back = slice(None, None, -1)
                ones = C("ones", 0, 1)[0:8].to_broadcast([8, T])
                scan = nc.vector.tensor_tensor_scan
                scan(r[3], ones, r[2], 0.0, ALU.mult, ALU.add)
                scan(r[10][:, back], ones, r[2][:, back], 0.0, ALU.mult, ALU.add)
                scan(r[8], r[2], r[0], 0.0, ALU.add, ALU.max)
                step(scan(r[9][:, back], r[2][:, back], r[0][:, back], 0.0, ALU.add, ALU.max))
                tt_(r[4], r[3], r[8], ALU.subtract)
                tt_(r[5], r[10], r[9], ALU.subtract)
                tt_(r[6], r[0], r[3], ALU.subtract)
                step(tt_(r[7], r[0], r[10], ALU.subtract), "ml_rows")
                dve.wait_ge(S["ml_tanh"], L + 1)
                step(stt(flat(ml_qk), flat(ml_th), 1.0, flat(ml_y), ALU.add, ALU.mult), "ml_qk")
                b = bank_of(dve, ("mlT", L))
                for k in range(4):
                    d = k % 2
                    dst = ml_col[:, :, 8 * (k // 2) + 2 * d:8 * (k // 2) + 2 * d + 2].rearrange("p h t -> p t h")
                    ins = cp(dst, b[:, k * 16:(k + 1) * 16].rearrange("p (t r) -> p t r", t=2)[:, :, 4 * d:4 * d + 4])
                step(ins, "ml_col")
                step(nc.vector.memset(ml_vt[:, :, :, HD:HD + 1], 1.0))
                dve.wait_ge(S["ml_em"], L + 1)
                dve.wait_ge(S["ml_v"], L + 1)
                dve.wait_ge(S["ml_o"], L + 1)
                step(ts(flat(ml_so), flat(ml_so), 0.5, 0.5, ALU.mult, ALU.add))

                def exponents(h):
                    b = bank_of(dve, ("mlG", L, h))
                    for d in range(2):
                        for st in range(2):
                            win = C("win", 3 * P * d + P * (1 - st), T)
                            ins = stt(ml_E[:, d, st, :], two(b)[:, d, :], ml_col[:, h, 2 * d + st:2 * d + st + 1], win,
                                      ALU.add, ALU.add)
                    step(ins, "ml_D")
                    dve.wait_ge(S["ml_E"], 4 * L + h + 1)
                    dve.wait_ge(S["ml_S"], 4 * L + h + 1)
                    pair = lambda a: a.rearrange("p a b c -> p a (b c)")
                    step(tt_(pair(ml_W), pair(ml_E), bc(flat(ml_S[:, h % 2, :, :]), 1, 2), ALU.mult), "ml_W")

                def read(h):
                    b = bank_of(dve, ("mlh", L, h))
                    v = b[:, 0:260].rearrange("p (n c) -> p n c", n=4)
                    dn = ml_dn[:, 0:4]
                    step(ts(ml_dn[:, 4:8], v[:, :, HD], -1.0, None, ALU.mult))
                    step(tt_(dn, ml_dn[:, 4:8], v[:, :, HD], ALU.max))
                    step(tt_(dn, dn, ml_em[:, h, :], ALU.max))
                    step(nc.vector.reciprocal(dn, dn))
                    for tt in range(TT):
                        ins = ts(ml_h[:, tt, h * HD:(h + 1) * HD], v[:, tt, 0:HD], dn[:, tt:tt + 1], None, ALU.mult)
                    step(ins)
                    for tt in range(TT):
                        ins = stt(ml_h[:, tt, h * HD:(h + 1) * HD], v[:, 2 + tt, 0:HD], dn[:, 2 + tt:3 + tt],
                                  ml_h[:, tt, h * HD:(h + 1) * HD], ALU.mult, ALU.add)
                    step(ins, "ml_h")

                for h in range(4):
                    exponents(h)
                    read(h)
                b = bank_of(dve, ("mlo", L))
                step(tt_(flat(brT[:, 3, :, :]), b[:, :], flat(ml_so), ALU.mult), "ml_done")

            def merge(L):
                for br in range(NBR):
                    for k in range(4):
                        b = bank_of(dve, ("br", L, br, k))
                        dve.wait_ge(S["mg_gate"], 16 * L + 4 * br + k + 1)
                        dst = flat(merged[:, 2 * k:2 * k + 2, :])
                        step(stt(dst if br == 0 else mg_t, mg_gate[:, k, :], 1.0, b[:, :], ALU.add, ALU.mult), "mg_sum")
                        if br:
                            step(tt_(dst, dst, mg_t, ALU.add), "mg_done" if br == NBR - 1 else None)

            def norm(k, sums, scale):
                dve.wait_ge(S["lnp_loaded"], 16 * (k + 1))
                for tt in range(TT):
                    for hf in range(2):
                        o = slice(hf * 512, (hf + 1) * 512)
                        step(ts(y_tok[:, tt, o], x_tok[:, tt, o], ALPHA / scale, None, ALU.mult))
                        src, name = sums(tt, hf)
                        step(tt_(y_tok[:, tt, o], y_tok[:, tt, o], src, ALU.add), name)
                        step(nc.vector.bn_stats(ln_bs[:, tt, hf, :], y_tok[:, tt, o]))
                    step(nc.vector.bn_aggr(ln_mv[:, tt, :], flat(ln_bs[:, tt, :, :])))
                step(ts(ln_mv[:, :, 1], ln_mv[:, :, 1], scale * scale, None, ALU.mult), "ln_sum")
                dve.wait_ge(S["ln_rs"], k + 1)
                step(ts(ln_rstd, ln_rstd, scale, None, ALU.mult))
                for tt in range(TT):
                    step(ts(x_tok[:, tt, :], y_tok[:, tt, :], ln_mv[:, tt, 0:1], ln_rstd[:, tt:tt + 1], ALU.subtract,
                            ALU.mult))
                    step(tt_(x_tok[:, tt, :], x_tok[:, tt, :], ln_gb[:, 0, :], ALU.mult))
                    step(tt_(x_tok[:, tt, :], x_tok[:, tt, :], ln_gb[:, 1, :], ALU.add), "ln_done")

            def gate_hidden(s, i, n, bank, before=None):
                dve.wait_ge(S["h_silu"], s + 1)
                if before is not None:
                    dve.wait_ge(S["unit_used"], s - 3 + before)
                tt_(ff_h[:, i, 0:n], ff_sl[:, i % 2, 0:n], bank[:, n:2 * n], ALU.mult).then_inc(S["h_ready"], 1)

            def dense():
                for s in range(4):
                    gate_hidden(s, s, T, banks[s % 2])
                with dve.Fori(4, 4 * (FF_STEPS // 4), 4) as s:
                    for i in range(4):
                        gate_hidden(s + i, i, T, banks[i % 2], used_before["dense"])
                for s in range(4 * (FF_STEPS // 4), FF_STEPS):
                    gate_hidden(s, s % 4, T, banks[s % 2], used_before["dense"])

            def router():
                b = bank_of(dve, ("route",))
                R = lambda k: ro[:, k, :]
                w2_ = lambda a: a.rearrange("p (t e) -> p t e", t=2)
                step(cp(R(1), b[:, 0:16]), "dve_freed")
                for tt in range(TT):
                    l = R(1)[:, tt * 8:tt * 8 + 8]
                    step(nc.vector.max(R(2)[:, tt * 8:tt * 8 + 8], l))
                    step(nc.vector.max_index(ro_idx[:, tt, :], R(2)[:, tt * 8:tt * 8 + 8], l))
                step(cp(R(3), ro_idx[:, :, :].rearrange("p a b -> p (a b)")))
                m, ix = w2_(R(2)), w2_(R(3))
                step(tt_(R(4)[:, 0:2], m[:, :, 1], m[:, :, 0], ALU.subtract), "ro_diff")
                dve.wait_ge(S["ro_exp"], 1)
                step(ts(R(5)[:, 0:2], R(4)[:, 0:2], 1.0, None, ALU.add))
                step(nc.vector.reciprocal(R(5)[:, 0:2], R(5)[:, 0:2]))
                step(tt_(R(5)[:, 2:4], R(4)[:, 0:2], R(5)[:, 0:2], ALU.mult))
                e8 = bc(C("e8"), 1, 2)
                step(tt_(w2_(R(6)), e8, bc(ix[:, :, 0], 2, NE), ALU.is_equal))
                step(tt_(w2_(R(7)), e8, bc(ix[:, :, 1], 2, NE), ALU.is_equal))
                step(tt_(w2_(R(8)), w2_(R(6)), bc(R(5)[:, 0:2], 2, NE), ALU.mult))
                step(tt_(w2_(R(9)), w2_(R(7)), bc(R(5)[:, 2:4], 2, NE), ALU.mult))
                step(tt_(R(8), R(8), R(9), ALU.add))
                step(tt_(R(0), R(6), R(7), ALU.add), "ro_done")
                b = bank_of(dve, ("rank",))
                step(cp(R(10), b[:, 0:16]))
                step(nc.vector.tensor_reduce(R(11)[:, 0:1], b[:, 16:24], AX, ALU.max), "dve_freed")
                step(ts(R(11)[:, 1:2], R(11)[:, 0:1], float(CAP), 1.0, ALU.is_gt, ALU.add))
                step(ts(R(11)[:, 2:3], R(11)[:, 0:1], float(2 * CAP), None, ALU.is_gt))
                step(tt_(R(11)[:, 1:2], R(11)[:, 1:2], R(11)[:, 2:3], ALU.add))
                step(nc.vector.memset(flat(acc), 0.0))
                step(cp(n_pass[:, :], R(11)[:, 1:2]), "passes_ready")

            def experts():
                passes = dve.value_load(n_pass[0:1, 0:1], min_val=1, max_val=3)
                h0 = FF_STEPS
                R = lambda k: ro[:, k, :]
                with dve.Fori(0, passes) as ps:
                    with dve.Fori(0, NE) as e:
                        it = dve.snap(ps * NE + e)
                        for tt in range(TT):
                            rank = R(10)[:, bass.ds(e + NE * tt, 1)]
                            ts(sel[:, tt, :], C("cap"), rank, R(0)[:, bass.ds(e + NE * tt, 1)], ALU.is_equal,
                               ALU.mult)
                            ins = ts(selw[:, tt, :], C("cap"), rank, R(8)[:, bass.ds(e + NE * tt, 1)],
                                     ALU.is_equal, ALU.mult)
                        ins.then_inc(S["sel_ready"], 1)
                        dve.wait_ge(S["sel_T"], it + 1)
                        cp(selwT[0:CAP, :], banks[6][0:CAP, 0:T]).then_inc(S["wT_ready"], 1)
                        for s in range(EX_STEPS):
                            gate_hidden(h0 + EX_STEPS * it + s, s % 4, CAP, banks[s % 2],
                                        used_before["experts"] - h0)
                        for k in range(4):
                            a, hf = k // 2, k % 2
                            dve.wait_ge(S["sc_filled"], 4 * it + k + 1)
                            o = acc[:, a, hf * 512:(hf + 1) * 512]
                            tt_(o, banks[4 + k % 2][:, :], o, ALU.add).then_inc(S["sc_added"], 1)
                    ts(R(10), R(10), float(CAP), None, ALU.subtract).then_inc(S["rank_moved"], 1)
                    dve.wait_ge(S["rank_moved"], ps + 1)
                dve.wait_ge(S["sc_added"], passes * (4 * NE))

            for L in range(DEPTH):
                if L == 0:
                    dve.wait_ge(S["cst_loaded"], 16)
                dve.wait_ge(S["par_loaded"], 32 * (L + 1))
                params(L)
                attention(L)
                rwkv(L)
                s5(L)
                mlstm(L)
                merge(L)

                def out_sums(tt, hf, L=L):
                    return bank_of(dve, ("out", L, 2 * tt + hf))[:, :], "dve_freed"
                norm(2 * L, out_sums, 0.5)
                if L == 0:
                    dense()
                    dve.wait_ge(S["unit_used"], used_before["dense"] + FF_STEPS)
                    norm(1, lambda tt, hf: (banks[2 + 2 * tt + hf][:, :], None), 1.0)
                else:
                    router()
                    experts()
                    norm(3, lambda tt, hf: (acc[:, tt, hf * 512:(hf + 1) * 512], None), 1.0)

        @block.sync
        def _(sp):
            def load(u, end=None):
                _, src, dst = stream[u]
                if u >= RING:
                    name, value = unit_end[u - RING]
                    sp.wait_ge(S[name], value)
                sp.dma_start(dst, src).then_inc(slot_loaded[u % RING], 16)

            sp.dma_start(x_tok[:, :, :], A["x"].rearrange("(a p) d -> p a d", p=P)).then_inc(S["x_loaded"], 16)
            u0, u1 = first_ff[0], first_ff[0] + FF_STEPS
            for s in range(FF_STEPS):
                unit_end[u0 + s] = ("unit_used", used_before["dense"] + s + 1)
            for u in range(u0 + 4):
                load(u)
            fours = A["ffn"][4:4 * (FF_STEPS // 4)].rearrange("(q i) p c -> q i p c", i=4)
            with sp.Fori(0, FF_STEPS // 4 - 1) as q:
                for i in range(4):
                    sp.wait_ge(S["unit_used"], used_before["dense"] + 4 * q + i + 1)
                    sp.dma_start(ring[:, i, :], fours[bass.ds(q, 1), i].rearrange("o p c -> p (o c)"))\
                        .then_inc(slot_loaded[i], 16)
            for u in range(u0 + 4 * (FF_STEPS // 4), first_ff[1]):
                load(u)
            for u in range(first_ff[1] - RING, first_ff[1]):
                sp.wait_ge(S[unit_end[u][0]], unit_end[u][1])
            sp.wait_ge(S["passes_ready"], 1)
            passes = sp.value_load(n_pass[0:1, 0:1], min_val=1, max_val=3)
            with sp.Fori(0, passes) as ps:
                with sp.Fori(0, NE) as e:
                    it = sp.snap(ps * NE + e)
                    for s in range(EX_STEPS):
                        i = (first_ff[1] + s) % RING
                        sp.wait_ge(S["unit_used"], used_before["experts"] - 3 + s + EX_STEPS * it)
                        sp.dma_start(ring[:, i, :], A["moe"][bass.ds(e, 1), s].rearrange("o p c -> p (o c)"))\
                            .then_inc(slot_loaded[i], 16)
            for tt in range(TT):
                sp.wait_ge(S["ln_done"], 7 + tt)
                sp.dma_start(A["out"][tt * P:(tt + 1) * P, :], x_tok[:, tt, :]).then_inc(S["stored"], 16)
            sp.wait_ge(S["stored"], 32)

        @block.gpsimd
        def _(pool):
            pool.dma_start(cst[:, :], A["cst"]).then_inc(S["cst_loaded"], 16)
            nc.gpsimd.memset(proj[:, :, 0:2], 0.0)
            nc.gpsimd.memset(proj[:, :, 2 + T:PITCH], 0.0).then_inc(S["pads_zeroed"], 1)
            for L in range(DEPTH):
                if L:
                    pool.wait_ge(S["ln_done"], 2)
                pool.dma_start(pv[:, :], A["pv"][L]).then_inc(S["par_loaded"], 16)
                pool.dma_start(pm[:, :], A["pm"][L]).then_inc(S["par_loaded"], 16)
                for k in (2 * L, 2 * L + 1):
                    if k % 2 == 0:
                        pool.wait_ge(S["ml_done"], L + 1)
                    else:
                        pool.wait_ge(S["ln_done"], 2 * k)
                    pool.dma_start(ln_gb[:, :, :], A["ln"][k].partition_broadcast(P)).then_inc(S["lnp_loaded"], 16)


def in_columns():
    c = np.full((NTILE, P), -1)
    rw, s5, mq, mv, mi, mo = 512, 1600, 1856, 2368, 2624, 2640
    r = np.arange(P)
    for i in range(2):
        c[Q0 + i] = np.where(r < 64, i * HD + r, (i + 2) * HD + r - 64)
    c[K0], c[V0] = 256 + r, 384 + r
    for i in range(6):
        c[R0 + i] = rw + i * P + r
    c[WD] = rw + 768 + r
    c[GL] = rw + 960 + r
    c[AIF, :64] = rw + 896 + r[:64]
    c[AIF, ROW_I:ROW_I + 8] = mi + r[:8]
    c[AIF, ROW_F:ROW_F + 8] = mi + 8 + r[:8]
    for i in range(2):
        c[U0 + i], c[MV0 + i], c[MO0 + i] = s5 + i * P + r, mv + i * P + r, mo + i * P + r
    for i in range(4):
        c[MQ0 + i] = mq + i * P + r
    return c


def tables(a):
    f = np.float32
    cols = in_columns()
    flat = cols.reshape(-1)
    hole = flat < 0

    def picked(x, axis_last):
        y = np.ascontiguousarray(x[..., np.where(hole, 0, flat)])
        y[..., hole] = 0
        return y

    w_in = picked(a["w_in"], True).reshape(DEPTH, KT, P, NTILE, P).transpose(0, 3, 2, 1, 4)
    out = {"w_in": w_in.reshape(DEPTH, NTILE, P, D)}
    out["w_gate"] = a["w_gate"].reshape(DEPTH, NBR, KT, P, KT, P).transpose(0, 1, 4, 3, 2, 5)\
        .reshape(DEPTH, NBR * KT, P, D)
    order = np.array([(i + 2 * b) * HD + d for i in range(2) for b in range(2) for d in range(HD)])
    wb = np.array(a["w_branch"])
    wb[:, 0] = wb[:, 0][:, order]
    out["w_branch"] = wb.reshape(DEPTH, NBR, 2, P, D).transpose(0, 1, 3, 2, 4)
    out["w_out"] = a["w_out"].reshape(DEPTH, 4, 2, P, D).transpose(0, 1, 3, 2, 4)

    def mlp(w1, w3, w2):
        n = w1.shape[-1] // P
        up = [w.reshape(KT, P, n, P).transpose(2, 1, 0, 3).reshape(n, P, D) for w in (w1, w3)]
        return np.concatenate(up + [w2.reshape(n, P, D)], 2)

    out["ffn"] = mlp(a["ffn_w1"][0], a["ffn_w3"][0], a["ffn_w2"][0])
    out["moe"] = np.stack([mlp(a["moe_w1"][0, e], a["moe_w3"][0, e], a["moe_w2"][0, e]) for e in range(NE)])
    out["ln"] = np.stack([np.stack([a[n + "_g"][L], a[n + "_b"][L]]) for L in range(DEPTH) for n in ("ln1", "ln2")])
    out["x"] = a["x"][0]
    out["cst"] = constants()

    pv = np.zeros((DEPTH, P, NPV), f)
    pm = np.zeros((DEPTH, P, NPM), f)
    for L in range(DEPTH):
        def put(name, x, table=pv, at=PV):
            o, n = at[name]
            table[L, :, o:o + n] = x

        def tiles(x):
            return x.reshape(-1, P).T

        put("b_in", tiles(picked(a["b_in"], True)[L]))
        gq, gk = (np.concatenate([g, g]) for g in (a["att_gq"][L], a["att_gk"][L]))
        put("gqk", np.stack([gq, gq, gk], 1))
        mix = np.zeros((2, 9, P), f)
        for k in range(2):
            m = a["rw_mix"][L, k]
            mix[k, 0:7] = m[0:896].reshape(7, P)
            mix[k, 7] = m[960:1088]
            mix[k, 8, 0:64] = m[896:960]
        put("mix", mix.reshape(18, P).T)
        put("w0", tiles(a["rw_w0"][L].reshape(-1)))
        for name, key in (("a0", "rw_a0"), ("kk", "rw_kk"), ("ka", "rw_ka"), ("rk", "rw_rk"), ("lng", "rw_ln_g"),
                          ("lnb", "rw_ln_b"), ("s5d", "s5_d"), ("glub", "s5_glu_b"), ("lre", "s5_lam_re"),
                          ("lim", "s5_lam_im"), ("convb", "ml_conv_b"), ("bgate", "b_gate")):
            put(name, tiles(a[key][L].reshape(-1)))
        put("ldt", tiles(np.repeat(a["s5_log_dt"][L].reshape(-1), 64)))
        put("convw", a["ml_conv_w"][L].reshape(5, 4, P).transpose(2, 1, 0).reshape(P, 20))
        ifb = np.zeros((P, 1), f)
        ifb[ROW_I:ROW_I + 8, 0] = a["ml_ib"][L].reshape(-1)
        ifb[ROW_F:ROW_F + 8, 0] = a["ml_fb"][L].reshape(-1)
        put("ifb", ifb)

        def mat(name, x):
            full = np.zeros((P, PM[name][1]), f)
            full[:x.shape[0]] = x
            put(name, full, pm, PM)

        mat("a2", a["rw_a2"][L])
        mat("g2", a["rw_g2"][L])
        mat("w2", a["rw_w2"][L].reshape(2 * 64, W))
        for name, key in (("bre", "s5_b_re"), ("bim", "s5_b_im")):
            m = np.zeros((P, 2 * P), f)
            for g in range(16):
                i = g // 2
                r, c = 16 * (g % 8), (i // 4) * P + 64 * (g % 2)
                m[r:r + 16, c:c + 64] = a[key][L, g].T
            mat(name, m)
        for name, key in (("cre", "s5_c_re"), ("cim", "s5_c_im")):
            m = np.zeros((P, 512), f)
            for d in range(2):
                for g in range(16):
                    i, h = g // 2, g % 2
                    c = (d * S5T + i) * 32 + 16 * h
                    m[64 * h:64 * h + 64, c:c + 16] = a[key][L, d, g].T
            mat(name, m)
        mat("glu", a["s5_glu_w"][L].reshape(2, P, W).transpose(1, 0, 2).reshape(P, 2 * W))
        mat("router", a["moe_router"][0].reshape(KT, P, NE).transpose(1, 0, 2).reshape(P, KT * NE))
    out["pv"], out["pm"] = pv, pm
    return {k: np.ascontiguousarray(v, dtype=f) for k, v in out.items()}


def kernel(**inputs):
    import concourse.bacc as bacc
    from concourse.bass_utils import run_bass_kernel_spmd as run

    data = tables({k: np.asarray(v) for k, v in inputs.items()})
    nc = bacc.Bacc("TRN2", target_bir_lowering=False, num_devices=1)
    A, arrays = {}, {}
    for name, a in data.items():
        arrays[f"in_{name}"] = a
        A[name] = nc.dram_tensor(f"in_{name}", a.shape, mybir.dt.from_np(a.dtype), kind="ExternalInput").ap()
    A["out"] = nc.dram_tensor("out_x", (T, D), F32, kind="ExternalOutput").ap()
    encoder(nc, A)
    r = run(nc, [arrays], core_ids=[0])
    return r.results[0]["out_x"].reshape(1, T, D)
```
